# Optimizing a Trainium2 kernel written in Bass

```python
import jax, jax.numpy as jnp
from jax import lax
import numpy as np

D_MODEL = 1024
BATCH = 1
SEQ = 256
DEPTH = 1

PLE_DIM = 256
MIX_WIDTH = D_MODEL
GDN_WIDTH = MIX_WIDTH // 2
HGRN_WIDTH = MIX_WIDTH - GDN_WIDTH
HEAD_DIM = 128
GDN_HEADS = GDN_WIDTH // HEAD_DIM
HGRN_HEADS = HGRN_WIDTH // HEAD_DIM
CONV_WIDTH = 4
GDN_CHUNK = 64
HGRN_CHUNK = 16
D_FF = 4 * D_MODEL
EPS = 1e-6

OFF_GDN_QKV = 0
OFF_GDN_Z = OFF_GDN_QKV + 3 * GDN_WIDTH
OFF_GDN_A = OFF_GDN_Z + GDN_WIDTH
OFF_GDN_B = OFF_GDN_A + GDN_HEADS
OFF_HG_F = OFF_GDN_B + GDN_HEADS
OFF_HG_I = OFF_HG_F + HGRN_WIDTH
OFF_HG_Q = OFF_HG_I + HGRN_WIDTH
OFF_HG_G = OFF_HG_Q + HGRN_WIDTH
IN_COLS = OFF_HG_G + HGRN_WIDTH


def rms_norm(x, w):
    xf = x.astype(jnp.float32)
    xf = xf * lax.rsqrt(jnp.mean(xf * xf, axis=-1, keepdims=True) + EPS)
    return (xf * w.astype(jnp.float32)).astype(x.dtype)

def gated_head_norm(o, w, z):
    o = o * lax.rsqrt(jnp.mean(o * o, axis=-1, keepdims=True) + EPS)
    return o * w.astype(jnp.float32) * jax.nn.silu(z)

def l2norm(t):
    return t * lax.rsqrt(jnp.sum(t * t, axis=-1, keepdims=True) + EPS)

def causal_depthwise_conv(x, w):
    k_w = w.shape[0]
    xp = jnp.pad(x, ((0, 0), (k_w - 1, 0), (0, 0)))
    return lax.conv_general_dilated(xp, w[:, None, :], window_strides=(1,), padding='VALID',
                                    dimension_numbers=('NWC', 'WIO', 'NWC'),
                                    feature_group_count=x.shape[-1])

def gated_delta_rule_chunked(q, k, v, g, beta):
    bsz, t_len, nh, dk = q.shape
    dv = v.shape[-1]
    c = GDN_CHUNK
    n = t_len // c
    q = q * (dk ** -0.5)
    q, k, v = (t.transpose(0, 2, 1, 3).reshape(bsz, nh, n, c, t.shape[-1]) for t in (q, k, v))
    g, beta = (t.transpose(0, 2, 1).reshape(bsz, nh, n, c) for t in (g, beta))
    gc = jnp.cumsum(g, axis=-1)
    causal = jnp.tril(jnp.ones((c, c), bool))
    strict = jnp.tril(jnp.ones((c, c), bool), -1)
    decay = jnp.exp(jnp.where(causal, gc[..., :, None] - gc[..., None, :], -jnp.inf))
    k_beta = k * beta[..., None]
    v_beta = v * beta[..., None]
    lmat = jnp.einsum('bhncd,bhnsd->bhncs', k_beta, k) * decay
    a_mat = jnp.eye(c, dtype=jnp.float32) + jnp.where(strict, lmat, 0.0)
    solve = lambda rhs: lax.linalg.triangular_solve(a_mat, rhs, left_side=True, lower=True,
                                                    unit_diagonal=True)
    u = solve(v_beta)
    w = solve(k_beta * jnp.exp(gc)[..., None])
    qk = jnp.einsum('bhncd,bhnsd->bhncs', q, k) * decay
    qg = q * jnp.exp(gc)[..., None]
    k_tail = k * jnp.exp(gc[..., -1:] - gc)[..., None]
    chunk_decay = jnp.exp(gc[..., -1])
    xs = tuple(jnp.moveaxis(t, 2, 0) for t in (u, w, qk, qg, k_tail, chunk_decay))

    def step(s, inp):
        u_n, w_n, qk_n, qg_n, kt_n, cd_n = inp
        v_new = u_n - jnp.einsum('bhcd,bhde->bhce', w_n, s)
        o = jnp.einsum('bhcd,bhde->bhce', qg_n, s) + jnp.einsum('bhcs,bhse->bhce', qk_n, v_new)
        s = s * cd_n[..., None, None] + jnp.einsum('bhcd,bhce->bhde', kt_n, v_new)
        return s, o

    s0 = jnp.zeros((bsz, nh, dk, dv), jnp.float32)
    _, o = lax.scan(step, s0, xs)
    return o.transpose(1, 0, 3, 2, 4).reshape(bsz, t_len, nh, dv)

def hgrn2_chunked(q, k, v, log_f):
    bsz, t_len, nh, dk = q.shape
    dv = v.shape[-1]
    c = HGRN_CHUNK
    n = t_len // c
    to_chunks = lambda t: jnp.moveaxis(t.reshape(bsz, n, c, nh, t.shape[-1]), 1, 0)
    bc = jnp.cumsum(to_chunks(log_f), axis=2)
    causal = jnp.tril(jnp.ones((c, c), bool))[None, :, :, None, None]

    def step(s, inp):
        q_n, k_n, v_n, b_n = inp
        pair = jnp.exp(jnp.where(causal, b_n[:, :, None] - b_n[:, None, :], -jnp.inf))
        att = jnp.einsum('bihd,bjhd,bijhd->bhij', q_n, k_n, pair)
        o = jnp.einsum('bhij,bjhe->bihe', att, v_n) + jnp.einsum('bihd,bhde->bihe', q_n * jnp.exp(b_n), s)
        b_last = b_n[:, -1]
        s = s * jnp.exp(b_last)[..., None] + jnp.einsum('bjhd,bjhe->bhde',
                                                         k_n * jnp.exp(b_last[:, None] - b_n), v_n)
        return s, o

    s0 = jnp.zeros((bsz, nh, dk, dv), jnp.float32)
    _, o = lax.scan(step, s0, (to_chunks(q), to_chunks(k), to_chunks(v), bc))
    return jnp.moveaxis(o, 0, 1).reshape(bsz, t_len, nh, dv)

def first_inputs(seed: int = 0) -> dict:
    key = jax.random.key(seed)
    ks = jax.random.split(key, 20)
    f32 = jnp.float32
    nrm = lambda k, shape, scale: scale * jax.random.normal(k, shape, f32)
    gain = lambda k, shape: 1.0 + 0.02 * jax.random.normal(k, shape, f32)
    return {
        'x': jax.random.normal(ks[0], (BATCH, SEQ, D_MODEL), f32),
        'p': jax.random.normal(ks[1], (DEPTH, BATCH, SEQ, PLE_DIM), f32),
        'pre_mix_norm': gain(ks[2], (DEPTH, D_MODEL)),
        'w_in': nrm(ks[3], (DEPTH, D_MODEL, IN_COLS), D_MODEL ** -0.5),
        'gdn_conv': nrm(ks[4], (DEPTH, CONV_WIDTH, 3 * GDN_WIDTH), CONV_WIDTH ** -0.5),
        'gdn_a_log': jnp.log(jax.random.uniform(ks[5], (DEPTH, GDN_HEADS), f32, 1.0, 16.0)),
        'gdn_dt_bias': nrm(ks[6], (DEPTH, GDN_HEADS), 0.1),
        'gdn_norm': gain(ks[7], (DEPTH, HEAD_DIM)),
        'hgrn_lb_logits': nrm(ks[8], (DEPTH, HGRN_WIDTH), 1.0),
        'hgrn_norm': gain(ks[9], (DEPTH, HEAD_DIM)),
        'w_out': nrm(ks[10], (DEPTH, MIX_WIDTH, D_MODEL), MIX_WIDTH ** -0.5),
        'post_mix_norm': gain(ks[11], (DEPTH, D_MODEL)),
        'pre_mlp_norm': gain(ks[12], (DEPTH, D_MODEL)),
        'w_mlp_up': nrm(ks[13], (DEPTH, D_MODEL, D_FF), D_MODEL ** -0.5),
        'w_mlp_down': nrm(ks[14], (DEPTH, D_FF, D_MODEL), D_FF ** -0.5),
        'post_mlp_norm': gain(ks[15], (DEPTH, D_MODEL)),
        'w_ple_proj': nrm(ks[16], (DEPTH, PLE_DIM, D_MODEL), PLE_DIM ** -0.5),
        'ple_norm': gain(ks[17], (DEPTH, D_MODEL)),
        'w_ple_gate': nrm(ks[18], (DEPTH, D_MODEL, D_MODEL), D_MODEL ** -0.5),
    }

def first_block(x, p, pre_mix_norm, w_in, gdn_conv, gdn_a_log, gdn_dt_bias, gdn_norm,
              hgrn_lb_logits, hgrn_norm, w_out, post_mix_norm, pre_mlp_norm, w_mlp_up,
              w_mlp_down, post_mlp_norm, w_ple_proj, ple_norm, w_ple_gate):
    f32 = jnp.float32
    bsz, t_len, _ = x.shape
    lb_cum = jnp.cumsum(jax.nn.softmax(hgrn_lb_logits.astype(f32), axis=0), axis=0)
    lower_bounds = lb_cum - lb_cum[0:1]
    h = x
    for i in range(DEPTH):
        hn = rms_norm(h, pre_mix_norm[i])
        proj = jnp.einsum('btd,dc->btc', hn, w_in[i]).astype(f32)
        qkv = proj[..., OFF_GDN_QKV:OFF_GDN_Z]
        z_gdn = proj[..., OFF_GDN_Z:OFF_GDN_A].reshape(bsz, t_len, GDN_HEADS, HEAD_DIM)
        a_gdn = proj[..., OFF_GDN_A:OFF_GDN_B]
        b_gdn = proj[..., OFF_GDN_B:OFF_HG_F]
        f_pre = proj[..., OFF_HG_F:OFF_HG_I].reshape(bsz, t_len, HGRN_HEADS, HEAD_DIM)
        i_hg = proj[..., OFF_HG_I:OFF_HG_Q].reshape(bsz, t_len, HGRN_HEADS, HEAD_DIM)
        q_hg = proj[..., OFF_HG_Q:OFF_HG_G].reshape(bsz, t_len, HGRN_HEADS, HEAD_DIM)
        g_hg = proj[..., OFF_HG_G:IN_COLS].reshape(bsz, t_len, HGRN_HEADS, HEAD_DIM)

        qkv = jax.nn.silu(causal_depthwise_conv(qkv, gdn_conv[i].astype(f32)))
        q_a, k_a, v_a = jnp.split(qkv, 3, axis=-1)
        q_a = l2norm(q_a.reshape(bsz, t_len, GDN_HEADS, HEAD_DIM))
        k_a = l2norm(k_a.reshape(bsz, t_len, GDN_HEADS, HEAD_DIM))
        v_a = v_a.reshape(bsz, t_len, GDN_HEADS, HEAD_DIM)
        beta = jax.nn.sigmoid(b_gdn)
        g_dec = -jnp.exp(gdn_a_log[i].astype(f32)) * jax.nn.softplus(a_gdn + gdn_dt_bias[i].astype(f32))
        o_a = gated_delta_rule_chunked(q_a, k_a, v_a, g_dec, beta)
        o_a = gated_head_norm(o_a, gdn_norm[i], z_gdn)

        lb = lower_bounds[i].reshape(HGRN_HEADS, HEAD_DIM)
        log_f = jnp.logaddexp(jax.nn.log_sigmoid(f_pre), jnp.log(lb) + jax.nn.log_sigmoid(-f_pre))
        k_b = (1.0 - lb) * jax.nn.sigmoid(-f_pre)
        o_b = hgrn2_chunked(jax.nn.silu(q_hg), k_b, i_hg, log_f)
        o_b = gated_head_norm(o_b, hgrn_norm[i], g_hg)

        mix = jnp.concatenate([o_a.reshape(bsz, t_len, GDN_WIDTH),
                               o_b.reshape(bsz, t_len, HGRN_WIDTH)], axis=-1).astype(h.dtype)
        mix_out = jnp.einsum('btc,cd->btd', mix, w_out[i])
        h = h + rms_norm(mix_out, post_mix_norm[i])

        u = jnp.einsum('btd,df->btf', rms_norm(h, pre_mlp_norm[i]), w_mlp_up[i])
        y = jnp.einsum('btf,fd->btd', jnp.square(jax.nn.relu(u)), w_mlp_down[i])
        h = h + rms_norm(y, post_mlp_norm[i])

        e = rms_norm(jnp.einsum('bte,ed->btd', p[i], w_ple_proj[i]), ple_norm[i])
        gate = jax.nn.sigmoid(jnp.einsum('btd,de->bte', h, w_ple_gate[i]))
        h = h + e * gate
    return h


N_META = 16
D_MIX = D_MODEL
D_SC = D_MIX // 2
D_CF = D_MIX - D_SC
N_GROUPS_SC = 8
N_GROUPS_CF = 8
SC_WIDTH = 3
CF_WIDTH = 31
D_IN = 3 * D_SC + 2 * D_CF
PEER_HEADS = 8
PEER_N_KEYS = 128
PEER_N_EXPERTS = PEER_N_KEYS * PEER_N_KEYS
PEER_D_KEY = 256
PEER_D_HALF = PEER_D_KEY // 2
PEER_TOPK = 16
PEER_CHUNK = 256


def rms_norm_2(x, g):
    xf = x.astype(jnp.float32)
    y = xf * lax.rsqrt(jnp.mean(xf * xf, axis=-1, keepdims=True) + EPS)
    return (y * g.astype(jnp.float32)).astype(x.dtype)

def layer_norm(x, g, b):
    xf = x.astype(jnp.float32)
    mu = jnp.mean(xf, axis=-1, keepdims=True)
    var = jnp.mean(jnp.square(xf - mu), axis=-1, keepdims=True)
    y = (xf - mu) * lax.rsqrt(var + EPS)
    return (y * g.astype(jnp.float32) + b.astype(jnp.float32)).astype(x.dtype)

def causal_depthwise_conv_2(x, w):
    k, c = w.shape
    return lax.conv_general_dilated(
        x, w[:, None, :].astype(x.dtype), window_strides=(1,), padding=[(k - 1, 0)],
        dimension_numbers=("NWC", "WIO", "NWC"), feature_group_count=c)

def short_conv_mixer(xv, bg, cg, w_conv):
    return bg * causal_depthwise_conv_2(cg * xv, w_conv)

def conformer_conv_mixer(a, gate, w_dw, b_dw, ln_g, ln_b):
    u = a * jax.nn.sigmoid(gate)
    u = causal_depthwise_conv_2(u, w_dw) + b_dw
    return jax.nn.silu(layer_norm(u, ln_g, ln_b))

def peer_route(q, sub_keys):
    s1 = jnp.einsum("thd,hnd->thn", q[..., :PEER_D_HALF], sub_keys[:, 0])
    s2 = jnp.einsum("thd,hnd->thn", q[..., PEER_D_HALF:], sub_keys[:, 1])
    v1, i1 = lax.top_k(s1, PEER_TOPK)
    v2, i2 = lax.top_k(s2, PEER_TOPK)
    cand = (v1[..., :, None] + v2[..., None, :]).reshape(q.shape[:-1] + (PEER_TOPK * PEER_TOPK,))
    vals, pos = lax.top_k(cand, PEER_TOPK)
    e1 = jnp.take_along_axis(i1, pos // PEER_TOPK, axis=-1)
    e2 = jnp.take_along_axis(i2, pos % PEER_TOPK, axis=-1)
    idx = e1 * PEER_N_KEYS + e2
    gates = jax.nn.softmax(vals.astype(jnp.float32), axis=-1).astype(q.dtype)
    return idx, gates

def peer_experts(xc, idx, gates, u, v):
    u_sel = jnp.take(u, idx, axis=0)
    act = jax.nn.gelu(jnp.einsum("chkd,cd->chk", u_sel, xc))
    v_sel = jnp.take(v, idx, axis=0)
    return jnp.einsum("chk,chkd->cd", act * gates, v_sel)

def peer_layer(x, w_q, sub_keys, u, v):
    b, t, d = x.shape
    n_tok = b * t
    pad = (-n_tok) % PEER_CHUNK
    xf = jnp.pad(x.reshape(n_tok, d), ((0, pad), (0, 0)))
    q = (xf @ w_q).reshape(n_tok + pad, PEER_HEADS, PEER_D_KEY)
    idx, gates = peer_route(q, sub_keys)
    n_chunks = (n_tok + pad) // PEER_CHUNK
    xc = xf.reshape(n_chunks, PEER_CHUNK, d)
    idxc = idx.reshape(n_chunks, PEER_CHUNK, PEER_HEADS, PEER_TOPK)
    gc = gates.reshape(n_chunks, PEER_CHUNK, PEER_HEADS, PEER_TOPK)
    out = lax.map(lambda args: peer_experts(args[0], args[1], args[2], u, v), (xc, idxc, gc))
    return out.reshape(n_tok + pad, d)[:n_tok].reshape(b, t, d)

def second_inputs(seed: int = 0) -> dict:
    key = jax.random.key(seed)
    ks = jax.random.split(key, 20)
    f32 = jnp.float32
    nrm = lambda k, shape, s: (jax.random.normal(k, shape, f32) * s)
    gain = lambda k, shape: 1.0 + 0.02 * jax.random.normal(k, shape, f32)
    return {
        "x": nrm(ks[0], (BATCH, SEQ, D_MODEL), 1.0),
        "meta_tokens": nrm(ks[1], (N_META, D_MODEL), 1.0),
        "norm_mix_g": gain(ks[2], (DEPTH, D_MODEL)),
        "w_in": nrm(ks[3], (DEPTH, D_MODEL, D_IN), D_MODEL ** -0.5),
        "sc_conv_w": nrm(ks[4], (DEPTH, SC_WIDTH, D_SC), SC_WIDTH ** -0.5),
        "cf_conv_w": nrm(ks[5], (DEPTH, CF_WIDTH, D_CF), CF_WIDTH ** -0.5),
        "cf_conv_b": nrm(ks[6], (DEPTH, D_CF), 0.02),
        "cf_ln_g": gain(ks[7], (DEPTH, D_CF)),
        "cf_ln_b": nrm(ks[8], (DEPTH, D_CF), 0.02),
        "out_norm_g_sc": gain(ks[9], (DEPTH, D_SC)),
        "out_norm_g_cf": gain(ks[10], (DEPTH, D_CF)),
        "w_out": nrm(ks[11], (DEPTH, D_MIX, D_MODEL), D_MIX ** -0.5),
        "norm_ffn_g": gain(ks[12], (DEPTH, D_MODEL)),
        "peer_w_q": nrm(ks[13], (DEPTH, D_MODEL, PEER_HEADS * PEER_D_KEY), D_MODEL ** -0.5),
        "peer_sub_keys": nrm(ks[14], (DEPTH, PEER_HEADS, 2, PEER_N_KEYS, PEER_D_HALF), PEER_D_HALF ** -0.5),
        "peer_u": nrm(ks[15], (DEPTH, PEER_N_EXPERTS, D_MODEL), D_MODEL ** -0.5),
        "peer_v": nrm(ks[16], (DEPTH, PEER_N_EXPERTS, D_MODEL), PEER_HEADS ** -0.5),
        "final_norm_g": gain(ks[17], (D_MODEL,)),
    }

def second_block(x, meta_tokens, norm_mix_g, w_in, sc_conv_w, cf_conv_w, cf_conv_b, cf_ln_g, cf_ln_b,
              out_norm_g_sc, out_norm_g_cf, w_out, norm_ffn_g, peer_w_q, peer_sub_keys, peer_u, peer_v,
              final_norm_g):
    b = x.shape[0]
    meta = jnp.broadcast_to(meta_tokens[None].astype(x.dtype), (b, N_META, x.shape[-1]))
    h = jnp.concatenate([meta, x], axis=1)
    splits = [D_SC, 2 * D_SC, 3 * D_SC, 3 * D_SC + D_CF]
    for l in range(DEPTH):
        hn = rms_norm_2(h, norm_mix_g[l])
        proj = hn @ w_in[l]
        xv, bg, cg, ga, gg = jnp.split(proj, splits, axis=-1)
        y_sc = short_conv_mixer(xv, bg, cg, sc_conv_w[l])
        y_cf = conformer_conv_mixer(ga, gg, cf_conv_w[l], cf_conv_b[l], cf_ln_g[l], cf_ln_b[l])
        y = jnp.concatenate([rms_norm_2(y_sc, out_norm_g_sc[l]), rms_norm_2(y_cf, out_norm_g_cf[l])], axis=-1)
        h = h + y @ w_out[l]
        hn = rms_norm_2(h, norm_ffn_g[l])
        h = h + peer_layer(hn, peer_w_q[l], peer_sub_keys[l], peer_u[l], peer_v[l])
    h = rms_norm_2(h, final_norm_g)
    return h[:, N_META:]


def setup_inputs(seed=0):
    out = dict(first_inputs(seed))
    for name, value in second_inputs(seed + 1).items():
        if name != "x":
            out[name + "_2"] = value
    return out


def reference(
    x, p, pre_mix_norm, w_in, gdn_conv, gdn_a_log, gdn_dt_bias, gdn_norm, hgrn_lb_logits,
    hgrn_norm, w_out, post_mix_norm, pre_mlp_norm, w_mlp_up, w_mlp_down, post_mlp_norm,
    w_ple_proj, ple_norm, w_ple_gate, meta_tokens_2, norm_mix_g_2, w_in_2, sc_conv_w_2,
    cf_conv_w_2, cf_conv_b_2, cf_ln_g_2, cf_ln_b_2, out_norm_g_sc_2, out_norm_g_cf_2, w_out_2,
    norm_ffn_g_2, peer_w_q_2, peer_sub_keys_2, peer_u_2, peer_v_2, final_norm_g_2,
):
    x = first_block(
        x, p, pre_mix_norm, w_in, gdn_conv, gdn_a_log, gdn_dt_bias, gdn_norm, hgrn_lb_logits,
        hgrn_norm, w_out, post_mix_norm, pre_mlp_norm, w_mlp_up, w_mlp_down, post_mlp_norm,
        w_ple_proj, ple_norm, w_ple_gate,
    )
    return second_block(
        x, meta_tokens_2, norm_mix_g_2, w_in_2, sc_conv_w_2, cf_conv_w_2, cf_conv_b_2,
        cf_ln_g_2, cf_ln_b_2, out_norm_g_sc_2, out_norm_g_cf_2, w_out_2, norm_ffn_g_2,
        peer_w_q_2, peer_sub_keys_2, peer_u_2, peer_v_2, final_norm_g_2,
    )


_drawn_inputs = setup_inputs


def setup_inputs(seed=0):
    import zlib

    import numpy as np

    out = dict(_drawn_inputs(seed))
    spreads = {}
    factors = {'gdn_a_log': 3.465,
     'gdn_dt_bias': 7.044,
     'gdn_norm': 3.982,
     'hgrn_norm': 3.323,
     'post_mix_norm': 2.894,
     'pre_mlp_norm': 3.158,
     'post_mlp_norm': 9.367,
     'ple_norm': 17.365,
     'norm_mix_g_2': 3.244,
     'cf_conv_b_2': 10.276,
     'cf_ln_g_2': 26.144,
     'cf_ln_b_2': 25.012,
     'out_norm_g_sc_2': 29.18,
     'out_norm_g_cf_2': 25.795,
     'norm_ffn_g_2': 19.804,
     'final_norm_g_2': 8.018}
    for name, (base, spread) in spreads.items():
        noise = np.random.default_rng([zlib.crc32(name.encode()), seed]).standard_normal(out[name].shape)
        drawn = base * np.exp(spread * noise) if base else spread * noise
        out[name] = __import__('jax').numpy.asarray(drawn.astype(out[name].dtype))
    for name, factor in factors.items():
        out[name] = (out[name] * factor).astype(out[name].dtype)
    return out
```

```python
from contextlib import ExitStack

import concourse.bass as bass
from concourse import mybir

F32 = mybir.dt.float32
U32 = mybir.dt.uint32
ALU = mybir.AluOpType
ACT = mybir.ActivationFunctionType
AX_X = mybir.AxisListType.X

P = 128
D = 1024
T = 256
NT = T // P
KD = D // P
HALF = 512
NH = 4
NC = NH * NT
META = 16
FF = 4096
EPS = 1e-6
SC_TAPS, CF_TAPS, GDN_TAPS = 3, 31, 4
NHH = 16
TOPK = 16
PEER_H = 8
N_KEYS = 128
LEVELS = 7
BIG = 1e30
LOWEST = -3.4028235e38

R = 8
TILES_FQ = 8
TILES_QKV = 12
TILES_ZI = 8
TILES_G = 4
TILES_OUT = 8
MLP_ROUNDS = FF // P // 8
G_QKV = TILES_FQ
G_ZI = G_QKV + TILES_QKV
G_G = G_ZI + TILES_ZI
G_OUT = G_G + TILES_G
G_MLP = G_OUT + TILES_OUT
G_PLE = G_MLP + MLP_ROUNDS * 16
G_GATE = G_PLE + 2
G_IN2 = G_GATE + 8
G_OUT2 = G_IN2 + 20
G_WQ = G_OUT2 + 8
G_KEYS = G_WQ + 16
G_PEER = G_KEYS + 2
G_END = G_PEER + 2 * N_KEYS
PEER_BODY = 4
PEER_ORDER = [("u", 0), ("u", 1), ("v", 0), ("u", 2), ("v", 1), ("u", 3), ("v", 2), ("v", 3)]
U_AT = [PEER_ORDER.index(("u", j)) for j in range(PEER_BODY)]
assert G_PEER % R == 0 and len(PEER_ORDER) == R

COLS = {}
_at = 0
for _name, _n in (("pre_mix", 8), ("head_norm", 2), ("pre_mlp", 8), ("mix2", 8), ("ffn2", 8),
                  ("gdn_conv", 12 * GDN_TAPS), ("sc_conv", 4 * SC_TAPS), ("cf_conv", 4 * CF_TAPS),
                  ("cf_b", 4), ("ln_g", 4), ("ln_b", 4), ("on_sc", 4), ("on_cf", 4)):
    COLS[_name] = _at
    _at += _n
NCOLS = _at

C_IDENT, C_ONES, C_TRI, C_LAST = 0, 128, 256, 384
C_MASK = 512
C_MASKT = C_MASK + LEVELS * P
C_BIAS = C_MASKT + LEVELS * P
C_BIAST = C_BIAS + P
C_IOTA = C_BIAST + P
C_IOTA16 = C_IOTA + P
C_NEGHALF = C_IOTA16 + 16
C_EPS = C_NEGHALF + 16
NCONST = C_EPS + 1


def two_stack_kernel(nc, x_in, pT_in, consts_in, cols_in, rows_in, small_in, wab_in, meta_in,
                     stream_in, out, dbg=None):
    ctx = ExitStack()
    with ctx:
        def sb(name, shape, dt=F32):
            return ctx.enter_context(nc.sbuf_tensor(name, shape, dt))

        def sem(name):
            return ctx.enter_context(nc.semaphore(name))

        ARENA = 32768
        arena = sb("arena", [P, ARENA])
        ring = sb("ring", [P, R, 1024])
        hT = sb("hT", [P, KD, META + T])
        h = sb("h", [P, NT, D])
        consts = sb("consts", [P, NCONST])
        cols = sb("cols", [P, NCOLS])
        stat = sb("stat", [P, 128])
        idxT = sb("idxT", [P, 3, T])
        onehot = sb("onehot", [P, 2, 4, 2, P])
        gel = sb("gel", [P, 2, T])
        wgt = sb("wgt", [P, PEER_BODY, T])
        metaT = sb("metaT", [P, KD, META])
        bank = [ctx.enter_context(nc.psum_tensor(f"bank{b}", [P, HALF], F32)) for b in range(8)]

        taken = [0]

        def area(*shape):
            n = 1
            for s in shape:
                n *= s
            a = arena[:, taken[0]:taken[0] + n]
            taken[0] += n
            assert taken[0] <= ARENA, taken[0]
            if len(shape) == 2:
                return a.rearrange("p (a b) -> p a b", a=shape[0])
            if len(shape) == 3:
                return a.rearrange("p (a b c) -> p a b c", a=shape[0], b=shape[1])
            if len(shape) == 4:
                return a.rearrange("p (a b c d) -> p a b c d", a=shape[0], b=shape[1], c=shape[2])
            return a

        normed = area(NT, D)
        rows = area(3, D)
        gates = area(NT, 2, HALF)
        taken_shared = taken[0]
        wab = area(KD, 8)
        ivals = area(NT, HALF)
        fgate_at = taken[0]
        fgate = area(NC, P)
        kdec = area(NC, P)
        qdec = area(NC, P)
        tot = area(NC * P)
        attT = area(NC, P)
        attX = area(NH, P)
        atmp = area(2, NC, P)
        conv = area(12, T)
        knT = area(NC, P)
        sq = area(8, T)
        vtok = area(NC, P)
        ktail = area(NH, P)
        decay = area(NC, P)
        decayT = area(NC, P)
        lmat = area(NC, P)
        xinv = area(NC, P)
        yinv = area(NC, P)
        lvl = area(NC, P)
        tsb = area(NC, P)
        diag = decay
        hg = fgate_at
        vnew = arena[:, hg:hg + D].rearrange("p (a b) -> p a b", a=2)
        rhs = arena[:, hg + D:hg + 2 * D].rearrange("p (a b) -> p a b", a=2)
        state = arena[:, hg + 2 * D:hg + 2 * D + HALF]
        qs = arena[:, hg + 2 * D + HALF:hg + 3 * D]
        osb = atmp.rearrange("p t c e -> p (t c e)").rearrange("p (t h e) -> p t h e", t=NT, h=8)
        taken[0] = taken_shared
        mid = area(8, T)
        relu = area(2, T)
        post = area(NT, D)
        emb = area(NT, D)
        pT = area(2, T)
        gsig = area(NT, D)
        hn_meta = area(D)
        meta_raw = gsig[:, 0, :]
        meta_junk = gsig[:, 1, :]
        sgate = area(2, META + T)
        upad = area(NH, META + T + 14)
        cfacc = area(NH, T)
        cgs = area(2, META + T)
        mconv = area(2, T + 2)
        scacc = area(NH, T)
        yT = area(KD, T)
        sq2 = area(NH, T)
        rstd2 = area(2, T)
        taken[0] = taken_shared
        qT = area(NHH, T)
        scores = area(NT, NHH, N_KEYS)
        scores2 = area(N_KEYS)
        vals = area(NT, NHH, TOPK)
        idx = area(NT, NHH, TOPK)
        idxf = area(NT, NHH, TOPK)
        cand = area(PEER_H, TOPK, TOPK)
        cand2 = area(256)
        top = area(NT, PEER_H, TOPK)
        pos = area(NT, PEER_H * TOPK)
        topx = area(PEER_H, TOPK)
        posh = area(PEER_H * TOPK)
        posf = area(2, PEER_H * TOPK)
        eq = area(PEER_H * TOPK, TOPK)
        picked = area(NT, 3, P)
        gmat = arena[:, :].rearrange("p (e t) -> p e t", t=T)

        ident = consts[:, C_IDENT:C_IDENT + P]
        ones = consts[:, C_ONES:C_ONES + P]
        iota = consts[:, C_IOTA:C_IOTA + P]
        iota16 = consts[:, C_IOTA16:C_IOTA16 + TOPK]
        neghalf = consts[:, C_NEGHALF:C_NEGHALF + 16]
        eps_col = consts[:, C_EPS:C_EPS + 1]

        osb_rows = osb.rearrange("p t h e -> p t (h e)")
        transposed = [normed, osb_rows, normed, h, normed, normed]
        block_cols = ["pre_mix", None, "pre_mlp", None, "mix2", "ffn2"]
        hT_at = [0, 0, 0, 0, META, 0]

        def conv_c(blk, c):
            return conv[:, blk + c // 2, (c % 2) * P:(c % 2 + 1) * P]

        def pair(buf, m):
            return buf[:, 2 * m:2 * m + 2, :].rearrange("p t n -> p (t n)")

        def cc(buf, c):
            return buf[:, c:c + 1]

        def quad(buf, b):
            return buf[:, 4 * b:4 * b + 4, :]

        def bank4(b):
            return bank[b][:, :].rearrange("p (c n) -> p c n", c=4)

        def over(a, n):
            return a.unsqueeze(1).to_broadcast([P, n, a.shape[-1]])

        def spread(a, n):
            return a.unsqueeze(2).to_broadcast([P, a.shape[-1], n])

        def col(name, i):
            return cols[:, COLS[name] + i:COLS[name] + i + 1]

        dtal = stat[:, 8:16]
        ab = stat[:, 16:32]
        sp = stat[:, 32:40]
        spx = stat[:, 40:48]
        spu = stat[:, 48:56]
        aexp = stat[:, 56:60]
        beta = stat[:, 60:68]
        gdec = stat[:, 68:76]
        gcum = stat[:, 76:84]
        ngcum = stat[:, 84:92]
        egc = stat[:, 92:100]
        tailc = stat[:, 100:104]
        negegc = stat[:, 104:112]
        rqk = stat[:, 112:128]
        mstat = sb("mstat", [P, 96])
        hsum = mstat[:, 0:16]
        hr = mstat[:, 16:32]
        gsum = mstat[:, 32:48].rearrange("p (t h) -> p t h", t=NT)
        grec = mstat[:, 48:64].rearrange("p (t h) -> p t h", t=NT)
        rqs = mstat[:, 64:72]
        ssq = [mstat[:, 72:76], mstat[:, 76:80]]
        ms = [mstat[:, 80:82], mstat[:, 82:84]]
        rstd = [mstat[:, 84:86], mstat[:, 86:88]]
        mss = mstat[:, 88:92]
        zeros = sb("zeros", [P, T])

        slot_full = [sem(f"slot_full{s}") for s in range(R)]
        tiles_done = sem("tiles_done")
        front_in = sem("front_in")
        side_in = sem("side_in")
        pT_loaded = sem("pT_loaded")
        zeroed = sem("zeroed")
        final_in = sem("final_in")
        out_done = sem("out_done")
        act_step, dve_step, pool_step = sem("act_step"), sem("dve_step"), sem("pool_step")
        ssq_done = sem("ssq_done")
        rstd_done = sem("rstd_done")
        normed_done = sem("normed_done")
        tr_full = sem("tr_full")
        tr_act, tr_dve = sem("tr_act"), sem("tr_dve")
        fq_out = sem("fq_out")
        conv_out = sem("conv_out")
        silu_out = sem("silu_out")
        z_out, i_out, g_out, ab_out = sem("z_out"), sem("i_out"), sem("g_out"), sem("ab_out")
        ab_full = sem("ab_full")
        kq_ready, att_full, att_out, att_sum = sem("kq_ready"), sem("att_full"), sem("att_out"), sem("att_sum")
        attx_full, attx_out, ob_full, ob_out = sem("attx_full"), sem("attx_out"), sem("ob_full"), sem("ob_out")
        sq_done, nsum_full, nsum_out, rqk_done = sem("sq_done"), sem("nsum_full"), sem("nsum_out"), sem("rqk_done")
        kdiag, kbc_full, kn_done = sem("kdiag"), sem("kbc_full"), sem("kn_done")
        sp_act, sp_dve, gdec_done = sem("sp_act"), sem("sp_dve"), sem("gdec_done")
        gcum_full, gcum_out, gcdiag, last_full, egc_done = (
            sem("gcum_full"), sem("gcum_out"), sem("gcdiag"), sem("last_full"), sem("egc_done"))
        grow_full, dbias, decays = sem("grow_full"), sem("dbias"), sem("decays")
        kk_full, kk_out, qk_full, qk_out = sem("kk_full"), sem("kk_out"), sem("qk_full"), sem("qk_out")
        vt_full, vt_out, kt_full, kt_out = sem("vt_full"), sem("vt_out"), sem("kt_full"), sem("kt_out")
        lvl_ready, t_full, t_out, d_full, xy_ready = (
            sem("lvl_ready"), sem("t_full"), sem("t_out"), sem("d_full"), sem("xy_ready"))
        r_ready, vn_full, vn_out, st_full, st_out = (
            sem("r_ready"), sem("vn_full"), sem("vn_out"), sem("st_full"), sem("st_out"))
        ks_full, oa_full, qs_out, oa_out = sem("ks_full"), sem("oa_full"), sem("qs_out"), sem("oa_out")
        hsq_done, hsum_done, hr_done = sem("hsq_done"), sem("hsum_done"), sem("hr_done")
        added = sem("added")
        relu_out, mid_out, mlp_full = sem("relu_out"), sem("mid_out"), sem("mlp_full")
        scaled_out, gsig_out = sem("scaled_out"), sem("gsig_out")
        meta_sq, meta_rstd, meta_n, meta_full, meta_out, meta_in_hT = (
            sem("meta_sq"), sem("meta_rstd"), sem("meta_n"), sem("meta_full"), sem("meta_out"), sem("meta_in_hT"))
        gg_out, u_out, cg_out, m_out, bg_out = sem("gg_out"), sem("u_out"), sem("cg_out"), sem("m_out"), sem("bg_out")
        cf_done, mean_full, cen_out, cen_sq, var_full, rs_act = (
            sem("cf_done"), sem("mean_full"), sem("cen_out"), sem("cen_sq"), sem("var_full"), sem("rs_act"))
        ln_out, ln_silu, y_sq, y_full, yT_out, sc_done = (
            sem("ln_out"), sem("ln_silu"), sem("y_sq"), sem("y_full"), sem("yT_out"), sem("sc_done"))
        qT_out, sc_full, sc_out, gate_in, gate_exp, picked_done = (
            sem("qT_out"), sem("sc_full"), sem("sc_out"), sem("gate_in"), sem("gate_exp"), sem("picked_done"))
        pk_full, pk_out, hot_ready, g_full, g_outs = (
            sem("pk_full"), sem("pk_out"), sem("hot_ready"), sem("g_full"), sem("g_outs"))
        u_full, gel_out, wgt_out, peer_full = sem("u_full"), sem("gel_out"), sem("wgt_out"), sem("peer_full")

        block = ctx.enter_context(nc.Block())


        @block.sync
        def _(sp_eng):
            for s in range(R):
                sp_eng.dma_start(ring[:, s, :], stream_in[s]).then_inc(slot_full[s], 16)
            with sp_eng.Fori(1, G_END // R) as i:
                for s in range(R):
                    sp_eng.wait_ge(tiles_done, i * R + (s - R + 1))
                    sp_eng.dma_start(ring[:, s, :], stream_in[bass.ds(i * R + s, 1), :, :].rearrange("a p n -> p (a n)"))\
                          .then_inc(slot_full[s], 16)
            sp_eng.wait_ge(normed_done, 2 * 6 + 2)
            sp_eng.dma_start(out.rearrange("b (t p) d -> p (b t) d", p=P), normed).then_inc(out_done, 16)
            sp_eng.wait_ge(out_done, 16)

        @block.tensor
        def _(pe):
            def tile(g):
                pe.wait_ge(slot_full[g % R], 16 * (g // R + 1))
                return ring[:, g % R, :]

            def transposes(n):
                src = transposed[n]
                for b in range(4):
                    pe.wait_ge(normed_done, 2 * n + 2)
                    for k in (2 * b, 2 * b + 1):
                        for t in range(NT):
                            o = (k % 2) * T + t * P
                            mm = nc.tensor.transpose(bank[b][:, o:o + P], src[:, t, k * P:(k + 1) * P], ident)
                    mm.then_inc(tr_full, 1)
                pe.wait_ge(tr_act, 4 * (n + 1))
                pe.wait_ge(tr_dve, 4 * (n + 1))

            def blocks(g0, n, off, width, free):
                for m in range(n):
                    w = tile(g0 + m)
                    free(m)
                    for k in range(KD):
                        mm = nc.tensor.matmul(bank[4 + (g0 + m) % 4][:, 0:width], w[:, k * P:(k + 1) * P],
                                              hT[:, k, off:off + width], start=(k == 0), stop=(k == KD - 1))
                    mm.then_inc(tiles_done, 1)

            def rows_out(g0, n, lhs, b0=0):
                for k in range(n):
                    w = tile(g0 + k)
                    for t in range(NT):
                        for c in range(2):
                            mm = nc.tensor.matmul(bank[b0 + 2 * t + c][:, :], lhs(k, t), w[:, c * HALF:(c + 1) * HALF],
                                                  start=(k == 0), stop=(k == n - 1))
                    mm.then_inc(tiles_done, 1)

            def hT_lhs(off):
                return lambda k, t: hT[:, k, off + t * P:off + (t + 1) * P]

            pe.wait_ge(meta_n, 1)
            for k in range(KD):
                mm = nc.tensor.transpose(bank[7][:, k * META:(k + 1) * META], hn_meta[0:META, k * P:(k + 1) * P],
                                         ident[0:META, 0:META])
            mm.then_inc(meta_full, 1)
            transposes(0)

            def free_a(m):
                if m < 4:
                    pe.wait_ge(meta_out, 1)
                elif m - 4 < 8:
                    pe.wait_ge(fq_out, m - 3)
                else:
                    pe.wait_ge(conv_out, m - 4 - 8 + 1)
            blocks(0, 20, 0, T, free_a)
            rows_out(G_ZI, 8, hT_lhs(0))
            pe.wait_ge(conv_out, 12)
            for k2 in range(4):
                w = tile(G_G + k2)
                for kk in range(2):
                    k = 2 * k2 + kk
                    for t in range(NT):
                        mm = nc.tensor.matmul(bank[4 + t][:, :], hT[:, k, t * P:(t + 1) * P],
                                              w[:, kk * HALF:(kk + 1) * HALF], start=(k == 0), stop=(k == KD - 1))
                mm.then_inc(tiles_done, 1)
            pe.wait_ge(side_in, 48)
            for t in range(NT):
                for k in range(KD):
                    mm = nc.tensor.matmul(bank[6][:, t * 8:(t + 1) * 8], hT[:, k, t * P:(t + 1) * P], wab[:, k, :],
                                          start=(k == 0), stop=(k == KD - 1))
            mm.then_inc(ab_full, 1)

            pe.wait_ge(z_out, 2)
            pe.wait_ge(i_out, 2)
            for l in range(LEVELS + 1):
                pe.wait_ge(kq_ready, l + 1)
                if l >= 2:
                    pe.wait_ge(att_out, l - 1)
                for c in range(NC):
                    b = 2 * (l % 2) + c // 4
                    mm = nc.tensor.matmul(bank[b][:, (c % 4) * P:(c % 4 + 1) * P], kdec[:, c, :], qdec[:, c, :],
                                          start=True, stop=True)
                mm.then_inc(att_full, 1)
            pe.wait_ge(kq_ready, LEVELS + 2)
            pe.wait_ge(att_out, LEVELS)
            for hd in range(NH):
                mm = nc.tensor.matmul(bank[0][:, hd * P:(hd + 1) * P], kdec[:, 2 * hd, :], qdec[:, 2 * hd + 1, :],
                                      start=True, stop=True)
            mm.then_inc(attx_full, 1)
            pe.wait_ge(attx_out, 1)
            pe.wait_ge(att_sum, LEVELS + 1)
            pe.wait_ge(att_out, LEVELS + 1)
            for hd in range(NH):
                v = [ivals[:, t, hd * P:(hd + 1) * P] for t in range(NT)]
                o = slice(hd * P, (hd + 1) * P)
                nc.tensor.matmul(bank[2][:, o], attT[:, 2 * hd, :], v[0], start=True, stop=True)
                nc.tensor.matmul(bank[3][:, o], attX[:, hd, :], v[0], start=True, stop=False)
                mm = nc.tensor.matmul(bank[3][:, o], attT[:, 2 * hd + 1, :], v[1], start=False, stop=True)
            mm.then_inc(ob_full, 1)

            pe.wait_ge(sq_done, 8)
            pe.wait_ge(ab_out, 1)
            for n in range(16):
                blk, t = n // 2, n % 2
                mm = nc.tensor.matmul(bank[6][:, n:n + 1], sq[:, blk, t * P:(t + 1) * P], ones[:, 0:1],
                                      start=True, stop=True)
            mm.then_inc(nsum_full, 1)
            pe.wait_ge(kdiag, 1)
            pe.wait_ge(g_out, 2)
            for b in range(2):
                mm = nc.tensor.matmul(bank[4 + b][:, :], ones, diag[:, 4 * b:4 * b + 4, :], start=True, stop=True)
            mm.then_inc(kbc_full, 1)
            pe.wait_ge(gdec_done, 1)
            pe.wait_ge(nsum_out, 1)
            nc.tensor.matmul(bank[7][:, 0:8], consts[:, C_TRI:C_TRI + P], gdec, start=True, stop=True)\
                .then_inc(gcum_full, 1)
            pe.wait_ge(gcum_out, 1)
            nc.tensor.matmul(bank[6][:, 0:8], consts[:, C_LAST:C_LAST + P], gcum, start=True, stop=True)\
                .then_inc(last_full, 1)
            pe.wait_ge(gcdiag, 1)
            pe.wait_ge(kn_done, 2)
            for b in range(2):
                mm = nc.tensor.matmul(bank[4 + b][:, :], ones, diag[:, 4 * b:4 * b + 4, :], start=True, stop=True)
            mm.then_inc(grow_full, 1)
            pe.wait_ge(attx_out, 1)
            pe.wait_ge(ob_out, 2)
            for c in range(NC):
                mm = nc.tensor.matmul(bank[c // 4][:, (c % 4) * P:(c % 4 + 1) * P], knT[:, c, :], knT[:, c, :],
                                      start=True, stop=True)
            mm.then_inc(kk_full, 1)
            for c in range(NC):
                mm = nc.tensor.matmul(bank[2 + c // 4][:, (c % 4) * P:(c % 4 + 1) * P], knT[:, c, :],
                                      conv_c(0, c), start=True, stop=True)
            mm.then_inc(qk_full, 1)
            pe.wait_ge(dbias, 2)
            for c in range(NC):
                mm = nc.tensor.transpose(bank[4 + c // 4][:, (c % 4) * P:(c % 4 + 1) * P], conv_c(8, c), ident)
            mm.then_inc(vt_full, 1)
            pe.wait_ge(egc_done, 1)
            for hd in range(NH):
                mm = nc.tensor.transpose(bank[6][:, hd * P:(hd + 1) * P], knT[:, 2 * hd, :], ident)
            mm.then_inc(kt_full, 1)
            pe.wait_ge(kk_out, 1)
            pe.wait_ge(vt_out, 1)
            pe.wait_ge(kt_out, 1)

            with pe.Fori(0, LEVELS) as i:
                pe.wait_ge(lvl_ready, i + 1)
                pe.wait_ge(xy_ready, i + 1)
                for c in range(NC):
                    mm = nc.tensor.matmul(bank[c // 4][:, (c % 4) * P:(c % 4 + 1) * P], lvl[:, c, :], yinv[:, c, :],
                                          start=True, stop=True)
                mm.then_inc(t_full, 1)
                pe.wait_ge(t_out, i + 2)
                for c in range(NC):
                    nc.tensor.matmul(bank[4 + c // 4][:, (c % 4) * P:(c % 4 + 1) * P], xinv[:, c, :], tsb[:, c, :],
                                     start=True, stop=True)
                    mm = nc.tensor.matmul(bank[6 + c // 4][:, (c % 4) * P:(c % 4 + 1) * P], tsb[:, c, :],
                                          xinv[:, c, :], start=True, stop=True)
                mm.then_inc(d_full, 1)
            pe.wait_ge(xy_ready, LEVELS + 1)
            pe.wait_ge(r_ready, 1)
            pe.wait_ge(qk_out, 1)

            def heads(b, lhs, rhs_of):
                for hd in range(NH):
                    mm = nc.tensor.matmul(bank[b][:, hd * P:(hd + 1) * P], lhs(hd), rhs_of(hd), start=True, stop=True)
                return mm

            def hcol(buf):
                return lambda hd: buf[:, hd * P:(hd + 1) * P]

            heads(0, lambda hd: yinv[:, 2 * hd, :], hcol(rhs[:, 0, :])).then_inc(vn_full, 1)
            pe.wait_ge(vn_out, 1)
            heads(2, lambda hd: ktail[:, hd, :], hcol(vnew[:, 0, :])).then_inc(st_full, 1)
            heads(1, lambda hd: decayT[:, 2 * hd, :], hcol(vnew[:, 0, :])).then_inc(oa_full, 1)
            pe.wait_ge(st_out, 1)
            heads(3, lambda hd: knT[:, 2 * hd + 1, :], hcol(state)).then_inc(ks_full, 1)
            heads(4, lambda hd: conv_c(0, 2 * hd + 1), hcol(state)).then_inc(ks_full, 1)
            pe.wait_ge(r_ready, 2)
            heads(0, lambda hd: yinv[:, 2 * hd + 1, :], hcol(rhs[:, 1, :])).then_inc(vn_full, 1)
            pe.wait_ge(vn_out, 2)
            heads(5, lambda hd: decayT[:, 2 * hd + 1, :], hcol(vnew[:, 1, :])).then_inc(oa_full, 1)

            transposes(1)
            rows_out(G_OUT, 8, hT_lhs(0))

            transposes(2)
            pe.wait_ge(zeroed, 1)
            zb = zeros[:, :].bitcast(mybir.dt.bfloat16)

            def open_sums(opening):
                for b in range(4):
                    mm = nc.tensor.matmul(bank[b][:, :], zb[:, 0:P], zb[:, 0:HALF], start=opening, stop=not opening)
                return mm

            open_sums(True)
            with pe.Fori(0, MLP_ROUNDS) as i:
                for m in range(8):
                    s = (G_MLP + m) % R
                    pe.wait_ge(slot_full[s], i * 32 + 16 * ((G_MLP + m) // R + 1))
                    pe.wait_ge(relu_out, i * 8 + m + 1)
                    for k in range(KD):
                        mm = nc.tensor.matmul(bank[4 + m % 4][:, 0:T], ring[:, s, k * P:(k + 1) * P], hT[:, k, 0:T],
                                              start=(k == 0), stop=(k == KD - 1))
                    mm.then_inc(tiles_done, 1)
                for m in range(8):
                    s = (G_MLP + m) % R
                    pe.wait_ge(slot_full[s], i * 32 + 16 * ((G_MLP + 8 + m) // R + 1))
                    pe.wait_ge(mid_out, i * 8 + m + 3)
                    for t in range(NT):
                        for c in range(2):
                            mm = nc.tensor.matmul(bank[2 * t + c][:, :], mid[:, m, t * P:(t + 1) * P],
                                                  ring[:, s, c * HALF:(c + 1) * HALF], start=False, stop=False)
                    mm.then_inc(tiles_done, 1)
            open_sums(False).then_inc(mlp_full, 1)

            pe.wait_ge(pT_loaded, 16)
            pe.wait_ge(relu_out, 4 + 8 * MLP_ROUNDS)
            rows_out(G_PLE, 2, lambda k, t: pT[:, k, t * P:(t + 1) * P], 4)
            transposes(3)
            rows_out(G_GATE, 8, hT_lhs(0))

            transposes(4)
            pe.wait_ge(meta_in_hT, 1)

            def taken_in2(j):
                if j < 8:
                    pe.wait_ge(gg_out if j % 2 == 0 else u_out, j // 2 + 1)
                else:
                    pe.wait_ge((cg_out, m_out, bg_out)[(j - 8) % 3], (j - 8) // 3 + 1)

            for m in range(20):
                w = tile(G_IN2 + m)
                if m >= 4:
                    taken_in2(m - 4)
                else:
                    pe.wait_ge(scaled_out, 12)
                off, width = (META, T) if m >= 8 and (m - 8) % 3 == 2 else (0, META + T)
                for k in range(KD):
                    mm = nc.tensor.matmul(bank[4 + m % 4][:, 0:width], w[:, k * P:(k + 1) * P],
                                          hT[:, k, off:off + width], start=(k == 0), stop=(k == KD - 1))
                mm.then_inc(tiles_done, 1)

            def column_sums(b, operand):
                for k in range(NH):
                    mm = nc.tensor.matmul(bank[b][:, 0:T], ones, operand[:, k, :], start=(k == 0), stop=(k == NH - 1))
                return mm

            pe.wait_ge(cf_done, NH)
            column_sums(0, cfacc).then_inc(mean_full, 1)
            pe.wait_ge(cen_sq, NH)
            column_sums(1, sq2).then_inc(var_full, 1)
            pe.wait_ge(y_sq, NH)
            column_sums(2, sq2).then_inc(y_full, 1)
            pe.wait_ge(y_sq, 2 * NH)
            column_sums(3, sq2).then_inc(y_full, 1)
            pe.wait_ge(yT_out, KD)
            rows_out(G_OUT2, 8, lambda k, t: yT[:, k, t * P:(t + 1) * P], 4)

            transposes(5)
            for m in range(NHH):
                w = tile(G_WQ + m)
                if m >= 4:
                    pe.wait_ge(qT_out, m - 3)
                for k in range(KD):
                    mm = nc.tensor.matmul(bank[4 + m % 4][:, 0:T], w[:, k * P:(k + 1) * P], hT[:, k, 0:T],
                                          start=(k == 0), stop=(k == KD - 1))
                mm.then_inc(tiles_done, 1)
            pe.wait_ge(qT_out, NHH)
            for n in range(2):
                w = tile(G_KEYS + n)
                for t in range(NT):
                    for q in range(8):
                        hh = 8 * n + q
                        mm = nc.tensor.matmul(bank[4 * t + hh // 4][:, (hh % 4) * P:(hh % 4 + 1) * P],
                                              qT[:, hh, t * P:(t + 1) * P], w[:, q * P:(q + 1) * P],
                                              start=True, stop=True)
                mm.then_inc(tiles_done, 1)
            pe.wait_ge(picked_done, NT)
            for j in range(3):
                for t in range(NT):
                    mm = nc.tensor.transpose(bank[j][:, t * P:(t + 1) * P], picked[:, t, j, :], ident)
            mm.then_inc(pk_full, 1)
            pe.wait_ge(pk_out, 1)
            with pe.Fori(0, T // 8) as i:
                for half in range(2):
                    pe.wait_ge(hot_ready, i * 2 + half + 1)
                    pe.wait_ge(g_outs, i * 2 + half + 1)
                    for n in range(4):
                        mm = nc.tensor.matmul(bank[half][:, n * P:(n + 1) * P], onehot[:, half, n, 1, :],
                                              onehot[:, half, n, 0, :], start=True, stop=True)
                    mm.then_inc(g_full, 1)
            pe.wait_ge(g_outs, 2 + T // 4)

            open_sums(True)
            with pe.Fori(0, N_KEYS // PEER_BODY) as i:
                for s, (kind, j) in enumerate(PEER_ORDER):
                    pe.wait_ge(slot_full[s], i * 16 + 16 * (G_PEER // R + 1))
                    if kind == "u":
                        for k in range(KD):
                            mm = nc.tensor.matmul(bank[4 + j][:, 0:T], ring[:, s, k * P:(k + 1) * P], hT[:, k, 0:T],
                                                  start=(k == 0), stop=(k == KD - 1))
                    else:
                        pe.wait_ge(wgt_out, i * PEER_BODY + j + 3)
                        for t in range(NT):
                            for c in range(2):
                                mm = nc.tensor.matmul(bank[2 * t + c][:, :], wgt[:, j, t * P:(t + 1) * P],
                                                      ring[:, s, c * HALF:(c + 1) * HALF], start=False, stop=False)
                    mm.then_inc(tiles_done, 1)
            open_sums(False).then_inc(peer_full, 1)

        @block.scalar
        def _(act):
            steps = [0]

            def link(ins):
                ins.then_inc(act_step, 1)
                steps[0] += 1
                act.wait_ge(act_step, steps[0])

            def squares(n, halves):
                if n:
                    act.wait_ge(ssq_done, 4 * n)
                for q, a in enumerate(halves):
                    nc.scalar.activation(normed[:, q // 2, (q % 2) * HALF:(q % 2 + 1) * HALF], a, ACT.Square,
                                         accum_out=ssq[n % 2][:, q:q + 1]).then_inc(ssq_done, 1)

            def halves(buf):
                return [buf[:, t, c * HALF:(c + 1) * HALF] for t in range(NT) for c in range(2)]

            def blocks_out(n):
                for k in range(4, KD):
                    if k % 2 == 0:
                        act.wait_ge(tr_full, 4 * n + k // 2 + 1)
                    src = bank[k // 2][:, (k % 2) * T:(k % 2 + 1) * T]
                    dst = hT[:, k, hT_at[n]:hT_at[n] + T]
                    sc = col("head_norm", 1) if n == 1 else (col(block_cols[n], k) if block_cols[n] else 1.0)
                    nc.scalar.activation(dst, src, ACT.Copy, scale=sc).then_inc(tr_act, 1)

            act.dma_start(consts[:, :], consts_in).then_inc(front_in, 16)
            act.dma_start(h[:, :, :], x_in.rearrange("b (t p) d -> p (b t) d", p=P)).then_inc(front_in, 16)
            act.dma_start(cols[:, :], cols_in).then_inc(front_in, 16)
            act.dma_start(meta_raw[0:META, :], meta_in).then_inc(front_in, 16)
            act.dma_start(wab, wab_in.rearrange("p (k n) -> p k n", k=KD)).then_inc(side_in, 16)
            act.dma_start(dtal, small_in.partition_broadcast(P)).then_inc(side_in, 16)
            act.dma_start(rows.rearrange("p a b -> p (a b)"), rows_in[0:1, 0:3 * D].rearrange("a n -> (a n)").partition_broadcast(P)).then_inc(side_in, 16)
            act.sem_inc(relu_out, 4)
            act.sem_inc(t_out, 1)
            act.sem_inc(g_outs, 2)
            act.wait_ge(front_in, 64)
            squares(0, halves(h))
            nc.scalar.activation(meta_junk[0:META, :], meta_raw[0:META, :], ACT.Square,
                                 accum_out=mss[0:META, 0:1]).then_inc(meta_sq, 1)
            blocks_out(0)
            for m in range(8):
                act.wait_ge(tiles_done, m + 1)
                src = bank[4 + m % 4][:, 0:T]
                if m < 4:
                    nc.scalar.activation(pair(fgate, m), src, ACT.Sigmoid)
                    nc.scalar.activation(pair(kdec, m), src, ACT.Sigmoid, scale=-1.0).then_inc(fq_out, 1)
                else:
                    nc.scalar.activation(pair(qdec, m - 4), src, ACT.Silu).then_inc(fq_out, 1)
            for m in range(12):
                act.wait_ge(conv_out, m + 1)
                nc.scalar.activation(conv[:, m, :], conv[:, m, :], ACT.Silu).then_inc(silu_out, 1)
            act.wait_ge(tiles_done, G_ZI + 8)
            for t in range(NT):
                nc.scalar.activation(gates[:, t, 0, :], bank[2 * t][:, :], ACT.Silu).then_inc(z_out, 1)
            act.wait_ge(tiles_done, G_G + 4)
            for t in range(NT):
                nc.scalar.activation(gates[:, t, 1, :], bank[4 + t][:, :], ACT.Silu).then_inc(g_out, 1)
            for m in range(8):
                act.wait_ge(silu_out, m + 1)
                nc.scalar.activation(sq[:, m, :], conv[:, m, :], ACT.Square).then_inc(sq_done, 1)
            act.wait_ge(sp_dve, 1)
            nc.scalar.activation(spx, spx, ACT.Exp).then_inc(sp_act, 1)
            nc.scalar.activation(aexp, dtal[:, 4:8], ACT.Exp).then_inc(sp_act, 1)
            nc.scalar.activation(beta, ab[:, 8:16], ACT.Exp, scale=-1.0).then_inc(sp_act, 1)
            act.wait_ge(sp_dve, 2)
            nc.scalar.activation(sp, spu, ACT.Ln).then_inc(sp_act, 1)
            act.wait_ge(gcum_out, 1)
            nc.scalar.activation(egc, gcum, ACT.Exp).then_inc(sp_act, 1)
            act.wait_ge(last_full, 1)
            act.wait_ge(gcdiag, 1)
            for hd in range(NH):
                ins = nc.scalar.activation(tailc[:, hd:hd + 1], bank[6][:, 2 * hd:2 * hd + 1], ACT.Exp,
                                           bias=cc(ngcum, 2 * hd))
            ins.then_inc(egc_done, 1)
            for b in range(2):
                act.wait_ge(dbias, b + 1)
                for c in range(4 * b, 4 * b + 4):
                    nc.scalar.activation(decay[:, c, :], tsb[:, c, :], ACT.Exp, scale=-1.0, bias=cc(gcum, c))
                    ins = nc.scalar.activation(decayT[:, c, :], lvl[:, c, :], ACT.Exp, bias=cc(ngcum, c))
                ins.then_inc(decays, 1)
            act.wait_ge(vt_full, 1)
            for b in range(2):
                ins = nc.scalar.activation(quad(vtok, b), bank4(4 + b), ACT.Copy)
            ins.then_inc(vt_out, 1)
            act.wait_ge(kt_full, 1)
            act.wait_ge(egc_done, 1)
            for hd in range(NH):
                ins = nc.scalar.activation(ktail[:, hd, :], bank[6][:, hd * P:(hd + 1) * P], ACT.Copy,
                                           scale=cc(tailc, hd))
            ins.then_inc(kt_out, 1)
            with act.Fori(0, LEVELS) as i:
                act.wait_ge(t_full, i + 1)
                nc.scalar.activation(quad(tsb, 0), bank4(0), ACT.Copy)
                nc.scalar.activation(quad(tsb, 1), bank4(1), ACT.Copy).then_inc(t_out, 1)
            act.wait_ge(st_full, 1)
            nc.scalar.activation(state, bank[2][:, :], ACT.Copy).then_inc(st_out, 1)
            act.wait_ge(ks_full, 2)
            for hd in range(NH):
                o = slice(hd * P, (hd + 1) * P)
                ins = nc.scalar.activation(qs[:, o], bank[4][:, o], ACT.Copy, scale=cc(egc, 2 * hd + 1))
            ins.then_inc(qs_out, 1)
            act.wait_ge(normed_done, 4)
            blocks_out(1)
            act.wait_ge(tiles_done, G_OUT + 8)
            squares(1, [bank[q][:, :] for q in range(4)])
            act.wait_ge(added, 2)
            squares(2, halves(h))
            act.dma_start(pT, pT_in.rearrange("p (k t) -> p k t", k=2)).then_inc(pT_loaded, 16)
            blocks_out(2)
            with act.Fori(0, MLP_ROUNDS) as i:
                for m in range(8):
                    act.wait_ge(tiles_done, i * 16 + (G_MLP + m + 1))
                    act.wait_ge(mid_out, i * 8 + m + 1)
                    nc.scalar.activation(relu[:, m % 2, :], bank[4 + m % 4][:, 0:T], ACT.Relu).then_inc(relu_out, 1)
            act.wait_ge(mlp_full, 1)
            squares(3, [bank[q][:, :] for q in range(4)])
            act.wait_ge(tiles_done, G_PLE + 2)
            squares(4, [bank[4 + q][:, :] for q in range(4)])
            blocks_out(3)
            act.wait_ge(tiles_done, G_GATE + 8)
            for t in range(NT):
                for c in range(2):
                    nc.scalar.activation(gsig[:, t, c * HALF:(c + 1) * HALF], bank[2 * t + c][:, :], ACT.Sigmoid)\
                        .then_inc(gsig_out, 1)
            act.wait_ge(added, 6)
            squares(5, halves(h))
            blocks_out(4)
            for b in range(NH):
                act.wait_ge(tiles_done, G_IN2 + 2 * b + 1)
                if b >= 2:
                    act.wait_ge(u_out, b - 1)
                nc.scalar.activation(sgate[:, b % 2, :], bank[4 + (2 * b) % 4][:, 0:META + T], ACT.Sigmoid)\
                    .then_inc(gg_out, 1)
            for b in range(NH):
                m = 8 + 3 * b
                act.wait_ge(tiles_done, G_IN2 + m + 1)
                if b >= 2:
                    act.wait_ge(m_out, b - 1)
                nc.scalar.activation(cgs[:, b % 2, :], bank[4 + m % 4][:, 0:META + T], ACT.Copy).then_inc(cg_out, 1)
            for b in range(NH):
                act.wait_ge(cen_out, b + 1)
                nc.scalar.activation(sq2[:, b, :], cfacc[:, b, :], ACT.Square).then_inc(cen_sq, 1)
            act.wait_ge(var_full, 1)
            nc.scalar.activation(rstd2[:, 0, :], bank[1][:, 0:T], ACT.Sqrt, scale=1.0 / HALF, bias=eps_col)\
                .then_inc(rs_act, 1)
            for b in range(NH):
                act.wait_ge(ln_out, b + 1)
                nc.scalar.activation(cfacc[:, b, :], cfacc[:, b, :], ACT.Silu, scale=col("ln_g", b),
                                     bias=col("ln_b", b)).then_inc(ln_silu, 1)
            act.wait_ge(ln_silu, NH)
            for b in range(NH):
                nc.scalar.activation(sq2[:, b, :], cfacc[:, b, :], ACT.Square).then_inc(y_sq, 1)
            act.wait_ge(y_full, 1)
            act.wait_ge(sc_done, NH)
            for b in range(NH):
                nc.scalar.activation(sq2[:, b, :], scacc[:, b, :], ACT.Square).then_inc(y_sq, 1)
            nc.scalar.activation(rstd2[:, 1, :], bank[2][:, 0:T], ACT.Sqrt, scale=1.0 / HALF, bias=eps_col)\
                .then_inc(rs_act, 1)
            act.wait_ge(y_full, 2)
            act.wait_ge(ln_out, NH)
            nc.scalar.activation(rstd2[:, 0, :], bank[3][:, 0:T], ACT.Sqrt, scale=1.0 / HALF, bias=eps_col)\
                .then_inc(rs_act, 1)
            act.wait_ge(added, 8)
            squares(6, halves(h))
            blocks_out(5)
            for m in range(NHH):
                act.wait_ge(tiles_done, G_WQ + m + 1)
                nc.scalar.activation(qT[:, m, :], bank[4 + m % 4][:, 0:T], ACT.Copy).then_inc(qT_out, 1)
            act.wait_ge(tiles_done, G_KEYS + 2)
            for b in range(8):
                nc.scalar.activation(scores[:, b // 4, 4 * (b % 4):4 * (b % 4) + 4, :], bank4(b), ACT.Copy)\
                    .then_inc(sc_out, 1)
            for t in range(NT):
                act.wait_ge(gate_in, t + 1)
                nc.scalar.activation(top[:, t, :, :], top[:, t, :, :], ACT.Exp).then_inc(gate_exp, 1)
            with act.Fori(0, T // 8) as i:
                for half in range(2):
                    act.wait_ge(g_full, i * 2 + half + 1)
                    nc.scalar.activation(gmat[:, :, bass.ds(i * 8 + 4 * half, 4)],
                                         bank[half][:, :].rearrange("p (n e) -> p e n", n=4), ACT.Copy)\
                        .then_inc(g_outs, 1)
            with act.Fori(0, N_KEYS // PEER_BODY) as i:
                for j in range(PEER_BODY):
                    act.wait_ge(tiles_done, i * 8 + (G_PEER + U_AT[j] + 1))
                    act.wait_ge(wgt_out, i * PEER_BODY + j + 1)
                    nc.scalar.activation(gel[:, j % 2, :], bank[4 + j][:, 0:T], ACT.Gelu_apprx_tanh)\
                        .then_inc(gel_out, 1)
            act.wait_ge(peer_full, 1)
            act.dma_start(rows[:, 0, :], rows_in[0:1, 3 * D:4 * D].rearrange("a n -> (a n)").partition_broadcast(P))\
               .then_inc(final_in, 16)
            act.wait_ge(added, 10)
            squares(7, halves(h))

        @block.gpsimd
        def _(pool):
            steps = [0]

            def link(ins):
                ins.then_inc(pool_step, 1)
                steps[0] += 1
                pool.wait_ge(pool_step, steps[0])

            def inv_rms(n):
                pool.wait_ge(ssq_done, 4 * (n + 1))
                q = ssq[n % 2].rearrange("p (t c) -> p t c", t=NT)
                link(nc.gpsimd.tensor_tensor(ms[n % 2], q[:, :, 0], q[:, :, 1], ALU.add))
                link(nc.gpsimd.tensor_scalar(ms[n % 2], ms[n % 2], 1.0 / D, EPS, ALU.mult, ALU.add))
                nc.gpsimd.tensor_tensor(rstd[n % 2], ms[n % 2], neghalf[:, 0:NT], ALU.pow).then_inc(rstd_done, 1)

            pool.wait_ge(front_in, 64)
            inv_rms(0)
            pool.wait_ge(meta_sq, 1)
            link(nc.gpsimd.tensor_scalar(mss[0:META, 1:2], mss[0:META, 0:1], 1.0 / D, EPS, ALU.mult, ALU.add))
            nc.gpsimd.tensor_tensor(mss[0:META, 2:3], mss[0:META, 1:2], neghalf[0:META, 0:1], ALU.pow)\
                .then_inc(meta_rstd, 1)
            for l in range(1, LEVELS + 1):
                pool.wait_ge(att_out, l + 1)
                pool.wait_ge(att_sum, l)
                nc.gpsimd.tensor_tensor(attT, attT, atmp[:, l % 2, :, :], ALU.add).then_inc(att_sum, 1)
            pool.wait_ge(nsum_out, 1)
            nc.gpsimd.tensor_tensor(rqk, rqk, neghalf, ALU.pow).then_inc(rqk_done, 1)
            with pool.Fori(0, LEVELS) as i:
                pool.wait_ge(kk_out, 1)
                pool.wait_ge(decays, 2)
                pool.wait_ge(t_out, i + 1)
                nc.gpsimd.tensor_tensor(lvl, lmat, consts[:, bass.ds(i * P + C_MASK, P)].unsqueeze(1).to_broadcast([P, NC, P]),
                                        ALU.mult).then_inc(lvl_ready, 1)
            pool.wait_ge(hsum_done, 1)
            link(nc.gpsimd.tensor_scalar(hsum, hsum, 1.0 / P, EPS, ALU.mult, ALU.add))
            nc.gpsimd.tensor_tensor(hr, hsum, neghalf, ALU.pow).then_inc(hr_done, 1)
            for n in range(1, 8):
                inv_rms(n)

        @block.vector
        def _(dve):
            steps = [0]

            def link(ins):
                ins.then_inc(dve_step, 1)
                steps[0] += 1
                dve.wait_ge(dve_step, steps[0])

            def normalise(n, stage):
                dve.wait_ge(rstd_done, n + 1)
                for t in range(NT):
                    nc.vector.tensor_scalar(normed[:, t, :], h[:, t, :], rstd[n % 2][:, t:t + 1], None, ALU.mult)\
                        .then_inc(normed_done, 1)

            def blocks_out(n):
                for k in range(4):
                    if k % 2 == 0:
                        dve.wait_ge(tr_full, 4 * n + k // 2 + 1)
                    src = bank[k // 2][:, (k % 2) * T:(k % 2 + 1) * T]
                    dst = hT[:, k, hT_at[n]:hT_at[n] + T]
                    sc = col("head_norm", 0) if n == 1 else (col(block_cols[n], k) if block_cols[n] else 1.0)
                    nc.vector.tensor_scalar(dst, src, sc, None, ALU.mult).then_inc(tr_dve, 1)

            def scaled_rows(n, b0, row, dst):
                dve.wait_ge(rstd_done, n + 1)
                for t in range(NT):
                    for c in range(2):
                        o = slice(c * HALF, (c + 1) * HALF)
                        ins = nc.vector.scalar_tensor_tensor(dst[:, t, o], bank[b0 + 2 * t + c][:, :],
                                                             rstd[n % 2][:, t:t + 1], rows[:, row, o], ALU.mult, ALU.mult)
                        ins.then_inc(scaled_out, 1)
                dve.wait_ge(scaled_out, 4 * {1: 1, 3: 2, 4: 3}[n])

            def add_rows(src):
                for t in range(NT):
                    nc.vector.tensor_tensor(h[:, t, :], h[:, t, :], src[:, t, :], ALU.add).then_inc(added, 1)

            nc.vector.memset(zeros[:, :], 0.0).then_inc(zeroed, 1)
            dve.wait_ge(front_in, 64)
            normalise(0, 0)
            dve.wait_ge(meta_rstd, 1)
            nc.vector.tensor_scalar(hn_meta[0:META, :], meta_raw[0:META, :], mss[0:META, 2:3], None, ALU.mult)\
                .then_inc(meta_n, 1)
            dve.wait_ge(meta_full, 1)
            link(nc.vector.tensor_copy(metaT[:, :, :], bank[7][:, 0:KD * META].rearrange("p (k n) -> p k n", k=KD)))
            nc.vector.tensor_tensor(metaT[:, :, :], metaT[:, :, :],
                                    spread(cols[:, COLS["mix2"]:COLS["mix2"] + KD], META), ALU.mult)\
                .then_inc(meta_out, 1)
            blocks_out(0)
            for m in range(12):
                dve.wait_ge(tiles_done, G_QKV + m + 1)
                src = bank[4 + (G_QKV + m) % 4][:, 0:T]
                w = COLS["gdn_conv"] + m * GDN_TAPS
                link(nc.vector.tensor_scalar(conv[:, m, :], src, cols[:, w + 3:w + 4], None, ALU.mult))
                for d in range(1, GDN_TAPS):
                    ins = nc.vector.scalar_tensor_tensor(conv[:, m, d:T], src[:, 0:T - d], cols[:, w + 3 - d:w + 4 - d],
                                                         conv[:, m, d:T], ALU.mult, ALU.add)
                    if d < GDN_TAPS - 1:
                        link(ins)
                ins.then_inc(conv_out, 1)
            dve.wait_ge(tiles_done, G_ZI + 8)
            for t in range(NT):
                nc.vector.tensor_copy(ivals[:, t, :], bank[2 * t + 1][:, :]).then_inc(i_out, 1)
            dve.wait_ge(ab_full, 1)
            for j in range(2):
                ins = nc.vector.tensor_copy(ab[:, 8 * j:8 * j + 8].rearrange("p (h t) -> p t h", t=NT),
                                            bank[6][:, 0:16].rearrange("p (t j h) -> p t j h", t=NT, j=2)[:, :, j, :])
            ins.then_inc(ab_out, 1)
            dve.wait_ge(fq_out, 8)
            dve.sem_inc(kq_ready, 1)
            f_all = fgate.rearrange("p c n -> p (c n)")
            k_all = kdec.rearrange("p c n -> p (c n)")
            q_all = qdec.rearrange("p c n -> p (c n)")
            t_from = f_all
            at = 0
            for l in range(LEVELS + 1):
                dve.wait_ge(att_full, l + 1)
                if l == 0:
                    nc.vector.tensor_tensor(q_all, q_all, f_all, ALU.mult).then_inc(kq_ready, 1)
                else:
                    s = 1 << (l - 1)
                    n = NC * P // (2 * s)
                    tv = t_from.rearrange("p (n two) -> p n two", two=2)
                    for buf, half, other in ((q_all, 1, 0), (k_all, 0, 1)):
                        v = buf.rearrange("p (n two s) -> p n two s", two=2, s=s)[:, :, half, :]
                        ins = nc.vector.tensor_tensor(v, v, tv[:, :, other].unsqueeze(2).to_broadcast([P, n, s]), ALU.mult)
                    ins.then_inc(kq_ready, 1)
                    if l < LEVELS:
                        t_to = tot[:, at:at + n]
                        link(nc.vector.tensor_tensor(t_to, tv[:, :, 0], tv[:, :, 1], ALU.mult))
                        t_from = t_to
                        at += n
                mask = ident if l == 0 else consts[:, C_MASKT + (l - 1) * P:C_MASKT + l * P]
                if l >= 3:
                    dve.wait_ge(att_sum, l - 1)
                dst = attT if l == 0 else atmp[:, l % 2, :, :]
                for b in range(2):
                    ins = nc.vector.tensor_tensor(quad(dst, b), bank4(2 * (l % 2) + b), over(mask, 4), ALU.mult)
                ins.then_inc(att_out, 1)
                if l == 0:
                    dve.wait_ge(att_out, 1)
                    dve.sem_inc(att_sum, 1)
            dve.wait_ge(attx_full, 1)
            nc.vector.tensor_copy(attX.rearrange("p h n -> p (h n)"), bank[0][:, :]).then_inc(attx_out, 1)
            dve.wait_ge(ob_full, 1)
            for t in range(NT):
                nc.vector.tensor_copy(osb[:, t, NH:8, :], bank4(2 + t)).then_inc(ob_out, 1)
            dve.wait_ge(ab_out, 1)
            dve.wait_ge(side_in, 48)
            link(nc.vector.tensor_tensor(ab[:, 0:8].rearrange("p (h t) -> p h t", t=NT),
                                         ab[:, 0:8].rearrange("p (h t) -> p h t", t=NT),
                                         spread(dtal[:, 0:4], NT), ALU.add))
            nc.vector.scalar_tensor_tensor(spx, ab[:, 0:8], -1.0, ab[:, 0:8], ALU.mult, ALU.min).then_inc(sp_dve, 1)
            dve.wait_ge(nsum_full, 1)
            nc.vector.tensor_scalar(rqk, bank[6][:, 0:16], EPS, None, ALU.add).then_inc(nsum_out, 1)
            dve.wait_ge(sp_act, 3)
            link(nc.vector.tensor_scalar(spu, spx, 1.0, None, ALU.add))
            dve.sem_inc(sp_dve, 1)
            link(nc.vector.tensor_scalar(beta, beta, 1.0, None, ALU.add))
            link(nc.vector.reciprocal(beta, beta))
            dve.wait_ge(sp_act, 4)
            link(nc.vector.tensor_scalar(spu, spu, -1.0, None, ALU.add))
            link(nc.vector.tensor_scalar(gdec, spu, 0.0, None, ALU.is_equal))
            link(nc.vector.tensor_tensor(sp, sp, gdec, ALU.add))
            link(nc.vector.tensor_tensor(spu, spu, gdec, ALU.add))
            link(nc.vector.reciprocal(spu, spu))
            link(nc.vector.tensor_tensor(sp, sp, spx, ALU.mult))
            link(nc.vector.tensor_tensor(sp, sp, spu, ALU.mult))
            link(nc.vector.scalar_tensor_tensor(sp, ab[:, 0:8], 0.0, sp, ALU.max, ALU.add))
            link(nc.vector.tensor_scalar(aexp, aexp, -1.0, None, ALU.mult))
            nc.vector.tensor_tensor(gdec.rearrange("p (h t) -> p h t", t=NT), sp.rearrange("p (h t) -> p h t", t=NT),
                                    spread(aexp, NT), ALU.mult).then_inc(gdec_done, 1)
            dve.wait_ge(rqk_done, 1)
            for c in range(NC):
                ins = nc.vector.tensor_scalar(diag[:, c, :], ident, rqk[:, 8 + c:9 + c], None, ALU.mult)
            ins.then_inc(kdiag, 1)
            dve.wait_ge(kbc_full, 1)
            dve.wait_ge(silu_out, 12)
            for b in range(2):
                nc.vector.tensor_tensor(quad(knT, b), conv[:, 4 + 2 * b:6 + 2 * b, :].rearrange("p m (t n) -> p (m t) n", t=NT),
                                        bank4(4 + b), ALU.mult).then_inc(kn_done, 1)
            dve.wait_ge(gcum_full, 1)
            link(nc.vector.tensor_copy(gcum, bank[7][:, 0:8]))
            dve.sem_inc(gcum_out, 1)
            nc.vector.tensor_scalar(ngcum, gcum, -1.0, None, ALU.mult)
            for c in range(NC):
                ins = nc.vector.tensor_scalar(diag[:, c, :], ident, cc(gcum, c), None, ALU.mult)
            ins.then_inc(gcdiag, 1)
            dve.wait_ge(grow_full, 1)
            for b in range(2):
                nc.vector.tensor_tensor(quad(tsb, b), bank4(4 + b), over(consts[:, C_BIAS:C_BIAS + P], 4), ALU.add)
                nc.vector.tensor_tensor(quad(lvl, b), bank4(4 + b), over(consts[:, C_BIAST:C_BIAST + P], 4),
                                        ALU.subtract).then_inc(dbias, 1)
            dve.wait_ge(kk_full, 1)
            dve.wait_ge(decays, 2)
            for b in range(2):
                link(nc.vector.tensor_tensor(quad(lmat, b), quad(decay, b), bank4(b), ALU.mult))
            nc.vector.tensor_tensor(lmat, lmat, spread(beta, P), ALU.mult).then_inc(kk_out, 1)
            dve.wait_ge(qk_full, 1)
            for b in range(2):
                ins = nc.vector.tensor_tensor(quad(decayT, b), quad(decayT, b), bank4(2 + b), ALU.mult)
            ins.then_inc(qk_out, 1)
            nc.vector.tensor_copy(xinv, over(ident, NC))
            nc.vector.tensor_copy(yinv, over(ident, NC)).then_inc(xy_ready, 1)
            dve.wait_ge(vt_out, 1)
            vh = vtok.rearrange("p (h t) n -> p t h n", t=NT)
            bh = beta.rearrange("p (h t) -> p t h", t=NT)
            rh = rhs.rearrange("p t (h n) -> p t h n", h=NH)
            nc.vector.tensor_tensor(rh[:, 0, :, :], vh[:, 0, :, :], spread(bh[:, 0, :], P), ALU.mult).then_inc(r_ready, 1)
            dve.wait_ge(sp_act, 5)
            nc.vector.tensor_scalar(negegc, egc, -1.0, None, ALU.mult)
            link(nc.vector.tensor_scalar(rqs, rqk[:, 0:8], float(P) ** -0.5, None, ALU.mult))
            with dve.Fori(0, LEVELS) as i:
                dve.wait_ge(d_full, i + 1)
                dve.wait_ge(xy_ready, i + 1)
                for b in range(2):
                    nc.vector.tensor_tensor(quad(yinv, b), quad(yinv, b), bank4(4 + b), ALU.subtract)
                    ins = nc.vector.tensor_tensor(quad(xinv, b), quad(xinv, b), bank4(6 + b), ALU.subtract)
                ins.then_inc(xy_ready, 1)
            dve.wait_ge(vn_full, 1)
            nc.vector.tensor_copy(vnew[:, 0, :], bank[0][:, :]).then_inc(vn_out, 1)
            dve.wait_ge(oa_full, 1)
            nc.vector.tensor_copy(osb[:, 0, 0:NH, :], bank4(1)).then_inc(oa_out, 1)
            dve.wait_ge(ks_full, 1)
            for hd in range(NH):
                c = 2 * hd + 1
                o = slice(hd * P, (hd + 1) * P)
                ins = nc.vector.scalar_tensor_tensor(rhs[:, 1, o], bank[3][:, o], cc(negegc, c), vtok[:, c, :],
                                                     ALU.mult, ALU.add)
                if hd == NH - 1:
                    link(ins)
            nc.vector.tensor_tensor(rh[:, 1, :, :], rh[:, 1, :, :], spread(bh[:, 1, :], P), ALU.mult).then_inc(r_ready, 1)
            dve.wait_ge(vn_full, 2)
            nc.vector.tensor_copy(vnew[:, 1, :], bank[0][:, :]).then_inc(vn_out, 1)
            dve.wait_ge(oa_full, 2)
            dve.wait_ge(qs_out, 1)
            nc.vector.tensor_tensor(osb[:, 1, 0:NH, :], bank4(5), qs.rearrange("p (h n) -> p h n", h=NH), ALU.add)\
                .then_inc(oa_out, 1)
            dve.wait_ge(oa_out, 2)
            rq = rqs.rearrange("p (h t) -> p t h", t=NT)
            for t in range(NT):
                link(nc.vector.tensor_tensor(osb[:, t, 0:NH, :], osb[:, t, 0:NH, :], spread(rq[:, t, :], P), ALU.mult))
            o16 = osb.rearrange("p t h e -> p (t h) e")
            dve.wait_ge(ob_out, 2)
            link(nc.vector.tensor_tensor(normed.rearrange("p t (h e) -> p (t h) e", e=P), o16, o16, ALU.mult))
            nc.vector.tensor_reduce(hsum, normed.rearrange("p t (h e) -> p (t h) e", e=P), axis=AX_X, op=ALU.add)\
                .then_inc(hsum_done, 1)
            dve.wait_ge(hr_done, 1)
            link(nc.vector.tensor_tensor(o16, o16, spread(hr, P), ALU.mult))
            dve.wait_ge(z_out, 2)
            dve.wait_ge(g_out, 2)
            for t in range(NT):
                nc.vector.tensor_tensor(osb_rows[:, t, :], osb_rows[:, t, :], gates[:, t, :, :].rearrange("p a b -> p (a b)"),
                                        ALU.mult).then_inc(normed_done, 1)
            blocks_out(1)
            scaled_rows(1, 0, 0, post)
            add_rows(post)
            dve.wait_ge(added, 2)
            normalise(2, 2)
            blocks_out(2)
            dve.sem_inc(mid_out, 2)
            with dve.Fori(0, MLP_ROUNDS) as i:
                for m in range(8):
                    dve.wait_ge(relu_out, i * 8 + m + 5)
                    nc.vector.tensor_tensor(mid[:, m, :], relu[:, m % 2, :], relu[:, m % 2, :], ALU.mult)\
                        .then_inc(mid_out, 1)
            scaled_rows(3, 0, 1, post)
            add_rows(post)
            for t in range(NT):
                dve.wait_ge(added, 3 + t)
                dve.sem_inc(normed_done, 1)
            scaled_rows(4, 4, 2, emb)
            blocks_out(3)
            dve.wait_ge(gsig_out, 4)
            for t in range(NT):
                link(nc.vector.tensor_tensor(emb[:, t, :], emb[:, t, :], gsig[:, t, :], ALU.mult))
            add_rows(emb)
            dve.wait_ge(tiles_done, G_GATE + 8)
            nc.vector.tensor_copy(hT[:, :, 0:META], metaT[:, :, :]).then_inc(meta_in_hT, 1)
            nc.vector.memset(upad[:, :, 0:14], 0.0)
            dve.wait_ge(added, 6)
            normalise(5, 4)
            blocks_out(4)
            for b in range(NH):
                m = 2 * b + 1
                dve.wait_ge(tiles_done, G_IN2 + m + 1)
                dve.wait_ge(gg_out, b + 1)
                nc.vector.tensor_tensor(upad[:, b, 14:14 + META + T], bank[4 + m % 4][:, 0:META + T], sgate[:, b % 2, :],
                                        ALU.mult).then_inc(u_out, 1)
                dve.wait_ge(u_out, b + 1)
                w = COLS["cf_conv"] + b * CF_TAPS
                link(nc.vector.tensor_scalar(cfacc[:, b, :], upad[:, b, 0:T], cols[:, w:w + 1], col("cf_b", b),
                                             ALU.mult, ALU.add))
                for k in range(1, CF_TAPS):
                    ins = nc.vector.scalar_tensor_tensor(cfacc[:, b, :], upad[:, b, k:k + T], cols[:, w + k:w + k + 1],
                                                         cfacc[:, b, :], ALU.mult, ALU.add)
                    if k < CF_TAPS - 1:
                        link(ins)
                ins.then_inc(cf_done, 1)
            for b in range(NH):
                m = 8 + 3 * b
                dve.wait_ge(tiles_done, G_IN2 + m + 2)
                dve.wait_ge(cg_out, b + 1)
                lead = META - 2
                nc.vector.tensor_tensor(mconv[:, b % 2, :], bank[4 + (m + 1) % 4][:, lead:META + T],
                                        cgs[:, b % 2, lead:META + T], ALU.mult).then_inc(m_out, 1)
                dve.wait_ge(m_out, b + 1)
                w = COLS["sc_conv"] + b * SC_TAPS
                link(nc.vector.tensor_scalar(scacc[:, b, :], mconv[:, b % 2, 0:T], cols[:, w:w + 1], None, ALU.mult))
                for k in range(1, SC_TAPS):
                    link(nc.vector.scalar_tensor_tensor(scacc[:, b, :], mconv[:, b % 2, k:k + T],
                                                        cols[:, w + k:w + k + 1], scacc[:, b, :], ALU.mult, ALU.add))
                dve.wait_ge(tiles_done, G_IN2 + m + 3)
                nc.vector.tensor_tensor(scacc[:, b, :], scacc[:, b, :], bank[4 + (m + 2) % 4][:, 0:T], ALU.mult)\
                    .then_inc(bg_out, 1)
            dve.wait_ge(cf_done, NH)
            dve.wait_ge(mean_full, 1)
            for b in range(NH):
                nc.vector.scalar_tensor_tensor(cfacc[:, b, :], bank[0][:, 0:T], -1.0 / HALF, cfacc[:, b, :],
                                               ALU.mult, ALU.add).then_inc(cen_out, 1)
            dve.wait_ge(rs_act, 1)
            link(nc.vector.reciprocal(rstd2[:, 0, :], rstd2[:, 0, :]))
            dve.wait_ge(cen_out, NH)
            dve.wait_ge(cen_sq, NH)
            for b in range(NH):
                nc.vector.tensor_tensor(cfacc[:, b, :], cfacc[:, b, :], rstd2[:, 0, :], ALU.mult).then_inc(ln_out, 1)
            dve.wait_ge(bg_out, NH)
            dve.sem_inc(sc_done, NH)
            for j, (acc, gain, at) in enumerate(((cfacc, "on_cf", 4), (scacc, "on_sc", 0))):
                r = rstd2[:, 1 - j, :]
                dve.wait_ge(rs_act, 2 + j)
                link(nc.vector.reciprocal(r, r))
                for b in range(NH):
                    nc.vector.scalar_tensor_tensor(yT[:, at + b, :], acc[:, b, :], col(gain, b), r, ALU.mult, ALU.mult)\
                        .then_inc(yT_out, 1)
            dve.wait_ge(tiles_done, G_OUT2 + 8)
            for t in range(NT):
                for c in range(2):
                    o = slice(c * HALF, (c + 1) * HALF)
                    ins = nc.vector.tensor_tensor(h[:, t, o], h[:, t, o], bank[4 + 2 * t + c][:, :], ALU.add)
                ins.then_inc(added, 1)
            dve.wait_ge(added, 8)
            normalise(6, 5)
            blocks_out(5)
            def top16(values, work, out_vals, out_idx):
                link(nc.vector.max(out_vals[:, 0:8], values))
                nc.vector.max_index(out_idx[:, 0:8].bitcast(U32), out_vals[:, 0:8], values)
                link(nc.vector.match_replace(work, out_vals[:, 0:8], values, LOWEST))
                link(nc.vector.max(out_vals[:, 8:16], work))
                link(nc.vector.max_index(out_idx[:, 8:16].bitcast(U32), out_vals[:, 8:16], work))

            for t in range(NT):
                for hh in range(NHH):
                    dve.wait_ge(sc_out, 4 * t + hh // 4 + 1)
                    top16(scores[:, t, hh, :], scores2, vals[:, t, hh, :], idx[:, t, hh, :])
                link(nc.vector.tensor_copy(idxf[:, t, :, :], idx[:, t, :, :].bitcast(U32)))
                two = vals[:, t, :, :].rearrange("p (h two) k -> p h two k", two=2)
                v1 = two[:, :, 0, :].unsqueeze(3).to_broadcast([P, PEER_H, TOPK, TOPK])
                v2 = two[:, :, 1, :].unsqueeze(2).to_broadcast([P, PEER_H, TOPK, TOPK])
                link(nc.vector.tensor_tensor(cand, v1, v2, ALU.add))
                for hd in range(PEER_H):
                    top16(cand[:, hd, :, :].rearrange("p a b -> p (a b)"), cand2, top[:, t, hd, :],
                          pos[:, t, hd * TOPK:(hd + 1) * TOPK])
                link(nc.vector.tensor_tensor(topx, top[:, t, :, :],
                                             top[:, t, :, 0:1].to_broadcast([P, PEER_H, TOPK]), ALU.subtract))
                nc.vector.tensor_copy(top[:, t, :, :], topx).then_inc(gate_in, 1)
                for j, (op, arg) in enumerate(((ALU.logical_shift_right, 4), (ALU.bitwise_and, 15))):
                    link(nc.vector.tensor_scalar(posh.bitcast(U32), pos[:, t, :].bitcast(U32), arg, None, op))
                    link(nc.vector.tensor_copy(posf[:, j, :], posh.bitcast(U32)))
                    link(nc.vector.tensor_tensor(eq, spread(posf[:, j, :], TOPK), over(iota16, PEER_H * TOPK), ALU.is_equal))
                    key = idxf[:, t, :, :].rearrange("p (h two) k -> p h two k", two=2)[:, :, j, :]
                    e4 = eq.rearrange("p (h k) n -> p h k n", h=PEER_H)
                    link(nc.vector.tensor_tensor(e4, e4, key.unsqueeze(2).to_broadcast([P, PEER_H, TOPK, TOPK]), ALU.mult))
                    link(nc.vector.tensor_reduce(picked[:, t, j, :], eq, axis=AX_X, op=ALU.add))
                dve.wait_ge(gate_exp, t + 1)
                link(nc.vector.tensor_reduce(gsum[:, t, :], top[:, t, :, :], axis=AX_X, op=ALU.add))
                link(nc.vector.reciprocal(grec[:, t, :], gsum[:, t, :]))
                nc.vector.tensor_tensor(picked[:, t, 2, :].rearrange("p (h k) -> p h k", h=PEER_H), top[:, t, :, :],
                                        spread(grec[:, t, :], TOPK), ALU.mult).then_inc(picked_done, 1)
            dve.wait_ge(pk_full, 1)
            for j in range(3):
                link(nc.vector.tensor_copy(idxT[:, j, :], bank[j][:, 0:T]))
            dve.sem_inc(pk_out, 1)
            with dve.Fori(0, T // 8) as i:
                for half in range(2):
                    dve.wait_ge(g_outs, i * 2 + half + 1)
                    for n in range(4):
                        at = i * 8 + (4 * half + n)
                        nc.vector.tensor_scalar(onehot[:, half, n, 0, :], iota, idxT[:, 0, bass.ds(at, 1)],
                                                idxT[:, 2, bass.ds(at, 1)], ALU.is_equal, ALU.mult)
                        ins = nc.vector.tensor_scalar(onehot[:, half, n, 1, :], iota, idxT[:, 1, bass.ds(at, 1)], None,
                                                      ALU.is_equal)
                    ins.then_inc(hot_ready, 1)
            dve.wait_ge(g_outs, 2 + T // 4)
            dve.sem_inc(wgt_out, 2)
            with dve.Fori(0, N_KEYS // PEER_BODY) as i:
                for j in range(PEER_BODY):
                    dve.wait_ge(gel_out, i * PEER_BODY + j + 1)
                    nc.vector.tensor_tensor(wgt[:, j, :], gel[:, j % 2, :],
                                            gmat[:, bass.ds(i * PEER_BODY + j, 1), :].rearrange("p a t -> p (a t)"),
                                            ALU.mult).then_inc(wgt_out, 1)
            dve.wait_ge(peer_full, 1)
            for t in range(NT):
                for c in range(2):
                    o = slice(c * HALF, (c + 1) * HALF)
                    ins = nc.vector.tensor_tensor(h[:, t, o], h[:, t, o], bank[2 * t + c][:, :], ALU.add)
                ins.then_inc(added, 1)
            dve.wait_ge(final_in, 16)
            dve.wait_ge(rstd_done, 8)
            for t in range(NT):
                nc.vector.scalar_tensor_tensor(normed[:, t, :], h[:, t, :], rstd[1][:, t:t + 1], rows[:, 0, :],
                                               ALU.mult, ALU.mult).then_inc(normed_done, 1)


def _constants(np):
    i = np.arange(P)
    c = np.zeros((P, NCONST), np.float32)
    c[:, C_IDENT:C_IDENT + P] = np.eye(P)
    c[:, C_ONES:C_ONES + P] = 1
    c[:, C_TRI:C_TRI + P] = i[:, None] <= i[None, :]
    c[:, C_LAST:C_LAST + P] = (i == P - 1)[:, None]
    for l in range(LEVELS):
        s = 1 << l
        m = (i[:, None] // (2 * s) == i[None, :] // (2 * s)) & (i[:, None] // s % 2 == 1) & (i[None, :] // s % 2 == 0)
        c[:, C_MASK + l * P:C_MASK + (l + 1) * P] = m
        c[:, C_MASKT + l * P:C_MASKT + (l + 1) * P] = m.T
    c[:, C_BIAS:C_BIAS + P] = np.where(i[None, :] > i[:, None], BIG, 0)
    c[:, C_BIAST:C_BIAST + P] = np.where(i[None, :] < i[:, None], BIG, 0)
    c[:, C_IOTA:C_IOTA + P] = i[None, :]
    c[:, C_IOTA16:C_IOTA16 + TOPK] = np.arange(TOPK)[None, :]
    c[:, C_NEGHALF:C_NEGHALF + 16] = -0.5
    c[:, C_EPS] = EPS
    return c


def _layout(np, a):
    def feature_blocks(w):
        return w.reshape(KD, P, -1, P).transpose(2, 1, 0, 3).reshape(-1, P, D)

    def per_feature(v):
        return v.reshape(-1, P).T

    w_in, w_in2 = a["w_in"][0], a["w_in_2"][0]
    o = {"qkv": 0, "z": 1536, "a": 2048, "f": 2056, "i": 2568, "q": 3080, "g": 3592}

    def part(name, n=HALF):
        return w_in[:, o[name]:o[name] + n]

    xv, bg, cg, ga, gg = (feature_blocks(w_in2[:, j * HALF:(j + 1) * HALF]) for j in range(5))
    stream = np.empty((G_END, P, D), np.float32)
    stream[0:4] = feature_blocks(part("f"))
    stream[4:8] = feature_blocks(part("q"))
    stream[G_QKV:G_ZI] = feature_blocks(part("qkv", 1536))
    stream[G_ZI:G_G, :, 0:HALF] = part("z").reshape(KD, P, HALF)
    stream[G_ZI:G_G, :, HALF:] = part("i").reshape(KD, P, HALF)
    stream[G_G:G_OUT] = part("g").reshape(4, 2, P, HALF).transpose(0, 2, 1, 3).reshape(4, P, D)
    stream[G_OUT:G_MLP] = a["w_out"][0].reshape(KD, P, D)
    mlp = stream[G_MLP:G_PLE].reshape(MLP_ROUNDS, 2, 8, P, D)
    mlp[:, 0] = feature_blocks(a["w_mlp_up"][0]).reshape(MLP_ROUNDS, 8, P, D)
    mlp[:, 1] = a["w_mlp_down"][0].reshape(MLP_ROUNDS, 8, P, D)
    stream[G_PLE:G_GATE] = a["w_ple_proj"][0].reshape(2, P, D)
    stream[G_GATE:G_IN2] = a["w_ple_gate"][0].reshape(KD, P, D)
    for b in range(NH):
        stream[G_IN2 + 2 * b], stream[G_IN2 + 2 * b + 1] = gg[b], ga[b]
        for n, w in enumerate((cg, xv, bg)):
            stream[G_IN2 + 8 + 3 * b + n] = w[b]
    stream[G_OUT2:G_WQ] = a["w_out_2"][0].reshape(KD, P, D)
    stream[G_WQ:G_KEYS] = feature_blocks(a["peer_w_q_2"][0])
    keys = a["peer_sub_keys_2"][0].reshape(NHH, N_KEYS, P).transpose(2, 0, 1).reshape(P, 2, D)
    stream[G_KEYS:G_PEER] = keys.transpose(1, 0, 2)
    peer = stream[G_PEER:].reshape(N_KEYS // PEER_BODY, R, P, D)
    u = a["peer_u_2"][0].reshape(N_KEYS // PEER_BODY, PEER_BODY, N_KEYS, KD, P)
    v = a["peer_v_2"][0].reshape(N_KEYS // PEER_BODY, PEER_BODY, N_KEYS, D)
    for s, (kind, j) in enumerate(PEER_ORDER):
        if kind == "u":
            peer[:, s] = u[:, j].transpose(0, 3, 2, 1).reshape(-1, P, D)
        else:
            peer[:, s] = v[:, j]

    def taps(w):
        return w.reshape(w.shape[0], -1, P).transpose(2, 1, 0).reshape(P, -1)

    cols = np.concatenate([
        per_feature(a["pre_mix_norm"][0]), a["gdn_norm"].T, a["hgrn_norm"].T, per_feature(a["pre_mlp_norm"][0]),
        per_feature(a["norm_mix_g_2"][0]), per_feature(a["norm_ffn_g_2"][0]), taps(a["gdn_conv"][0]),
        taps(a["sc_conv_w_2"][0]), taps(a["cf_conv_w_2"][0]), per_feature(a["cf_conv_b_2"][0]),
        per_feature(a["cf_ln_g_2"][0]), per_feature(a["cf_ln_b_2"][0]), per_feature(a["out_norm_g_sc_2"][0]),
        per_feature(a["out_norm_g_cf_2"][0])], axis=1)
    rows = np.concatenate([a["post_mix_norm"], a["post_mlp_norm"], a["ple_norm"], a["final_norm_g_2"][None]], axis=1)
    return {
        "x": a["x"],
        "pT": a["p"][0, 0].reshape(T, 2, P).transpose(2, 1, 0).reshape(P, 2 * T),
        "consts": _constants(np),
        "cols": cols,
        "rows": rows,
        "small": np.concatenate([a["gdn_dt_bias"][0], a["gdn_a_log"][0]]),
        "wab": part("a", 8).reshape(KD, P, 8).transpose(1, 0, 2).reshape(P, 64),
        "meta": a["meta_tokens_2"],
        "stream": stream,
    }


def kernel(**inputs):
    import numpy as np
    import concourse.bacc as bacc
    from concourse.bass_utils import run_bass_kernel_spmd

    nc = bacc.Bacc("TRN2", target_bir_lowering=False, num_devices=1)
    arrays, args = {}, []
    for name, v in _layout(np, {k: np.asarray(v) for k, v in inputs.items()}).items():
        v = np.ascontiguousarray(v)
        arrays[f"in_{name}"] = v
        args.append(nc.dram_tensor(f"in_{name}", v.shape, F32, kind="ExternalInput").ap())
    out = nc.dram_tensor("out_h", (1, T, D), F32, kind="ExternalOutput").ap()
    two_stack_kernel(nc, *args, out)
    r = run_bass_kernel_spmd(nc, [arrays], core_ids=[0])
    return r.results[0]["out_h"]
```
